# Optimizing a Trainium2 kernel written in Bass

```python
import jax, jax.numpy as jnp
from jax import lax
import numpy as np

D_MODEL = 1024
BATCH = 1
SEQ = 512
DEPTH = 2

D_MIX = D_MODEL
POOL_WINDOWS = (2, 4, 8, 16)
POOL_GROUPS = len(POOL_WINDOWS)
POOL_WIDTH = D_MIX // 4
POOL_CH = POOL_WIDTH // POOL_GROUPS
SG_HEADS = 4
SG_WIDTH = D_MIX // 4
SG_DIM = SG_WIDTH // SG_HEADS
SG_CHUNK = 128
MLA_HEADS = 8
MLA_WIDTH = D_MIX - POOL_WIDTH - SG_WIDTH
V_DIM = MLA_WIDTH // MLA_HEADS
QK_NOPE = 64
QK_ROPE = 32
Q_LORA = D_MODEL // 4
KV_LORA = D_MODEL // 8
ROPE_THETA = 10000.0
Q_BLOCK = 128
ATTN_SCALE = (QK_NOPE + QK_ROPE) ** -0.5
IN_SPLITS = (POOL_WIDTH,
             POOL_WIDTH + SG_WIDTH,
             POOL_WIDTH + 2 * SG_WIDTH,
             POOL_WIDTH + 2 * SG_WIDTH + Q_LORA,
             POOL_WIDTH + 2 * SG_WIDTH + Q_LORA + KV_LORA)
N_IN = POOL_WIDTH + 2 * SG_WIDTH + Q_LORA + KV_LORA + QK_ROPE
N_EXPERTS = 64
TOP_K = 8
N_EXPERT_GROUPS = 8
TOPK_GROUPS = 4
EXPERT_FF = D_MODEL // 4
SHARED_FF = EXPERT_FF
ROUTED_SCALE = 2.5
EXPERT_BLOCK = 128
EPS = 1e-6
MAX_POS_OFFSET = 1024

kernel_name = 'hymba_pool_sgu_mla_moe_adaln'

def _rms_norm(x, gain=None):
    xf = x.astype(jnp.float32)
    y = xf * lax.rsqrt(jnp.mean(xf * xf, axis=-1, keepdims=True) + EPS)
    if gain is not None:
        y = y * gain.astype(jnp.float32)
    return y.astype(x.dtype)

def _ada_norm(x, shift, scale):
    return _rms_norm(x) * (1 + scale) + shift

def _pool_mixer(a, w_pool, pool_scale):
    b, s, _ = a.shape
    af = a.astype(jnp.float32)
    csum = jnp.cumsum(af, axis=1)
    t = jnp.arange(1, s + 1, dtype=jnp.float32)[:, None]
    means = []
    for g, w in enumerate(POOL_WINDOWS):
        cg = csum[..., g * POOL_CH:(g + 1) * POOL_CH]
        lag = jnp.pad(cg, ((0, 0), (w, 0), (0, 0)))[:, :s]
        means.append((cg - lag) / jnp.minimum(t, float(w)))
    d = (jnp.stack(means, axis=2) - af.reshape(b, s, POOL_GROUPS, POOL_CH)).astype(a.dtype)
    y = jnp.einsum('bsgc,gcd->bsgd', d, w_pool).reshape(b, s, POOL_WIDTH)
    return y * pool_scale

def _spatial_gating(u, v, w_spatial, b_spatial):
    b, s, _ = u.shape
    u = jax.nn.gelu(u)
    vf = jax.nn.gelu(v).astype(jnp.float32)
    mu = jnp.mean(vf, axis=-1, keepdims=True)
    var = jnp.mean(jnp.square(vf - mu), axis=-1, keepdims=True)
    vn = ((vf - mu) * lax.rsqrt(var + EPS)).astype(v.dtype)
    vn = vn.reshape(b, s // SG_CHUNK, SG_CHUNK, SG_HEADS, SG_DIM)
    causal = jnp.tril(jnp.ones((SG_CHUNK, SG_CHUNK), w_spatial.dtype))
    mixed = jnp.einsum('htk,bnkhd->bnthd', w_spatial * causal, vn) + b_spatial.T[:, :, None]
    return u * mixed.reshape(b, s, SG_WIDTH)

def _rope(x, cos, sin):
    half = x.shape[-1] // 2
    xf = x.astype(jnp.float32)
    x1, x2 = xf[..., :half], xf[..., half:]
    return jnp.concatenate([x1 * cos - x2 * sin, x2 * cos + x1 * sin], axis=-1).astype(x.dtype)

def _latent_attention(cq, ckv, k_pe, positions, g_q, w_uq, g_kv, w_ukv):
    b, s, _ = cq.shape
    q = (_rms_norm(cq, g_q) @ w_uq).reshape(b, s, MLA_HEADS, QK_NOPE + QK_ROPE)
    kv = (_rms_norm(ckv, g_kv) @ w_ukv).reshape(b, s, MLA_HEADS, QK_NOPE + V_DIM)
    q_nope, q_pe = q[..., :QK_NOPE], q[..., QK_NOPE:]
    k_nope, v = kv[..., :QK_NOPE], kv[..., QK_NOPE:]
    inv_freq = ROPE_THETA ** (-jnp.arange(0, QK_ROPE, 2, dtype=jnp.float32) / QK_ROPE)
    ang = positions.astype(jnp.float32)[..., None] * inv_freq
    cos, sin = jnp.cos(ang), jnp.sin(ang)
    q_pe = _rope(q_pe, cos[:, :, None], sin[:, :, None])
    k_pe = _rope(k_pe, cos, sin)
    outs = []
    for i in range(s // Q_BLOCK):
        q0, k_end = i * Q_BLOCK, (i + 1) * Q_BLOCK
        scores = (jnp.einsum('bqhd,bkhd->bhqk', q_nope[:, q0:k_end], k_nope[:, :k_end])
                  + jnp.einsum('bqhr,bkr->bhqk', q_pe[:, q0:k_end], k_pe[:, :k_end])
                  ).astype(jnp.float32) * ATTN_SCALE
        causal = jnp.arange(k_end)[None, :] <= (q0 + jnp.arange(Q_BLOCK))[:, None]
        probs = jax.nn.softmax(jnp.where(causal, scores, -jnp.inf), axis=-1).astype(v.dtype)
        outs.append(jnp.einsum('bhqk,bkhd->bqhd', probs, v[:, :k_end]))
    return jnp.concatenate(outs, axis=1).reshape(b, s, MLA_WIDTH)

def _token_mixer(h, positions, w_in, w_pool, pool_scale, w_spatial, b_spatial,
                 g_q, w_uq, g_kv, w_ukv, w_out):
    a, u, v, cq, ckv, k_pe = jnp.split(h @ w_in, IN_SPLITS, axis=-1)
    y = jnp.concatenate([
        _pool_mixer(a, w_pool, pool_scale),
        _spatial_gating(u, v, w_spatial, b_spatial),
        _latent_attention(cq, ckv, k_pe, positions, g_q, w_uq, g_kv, w_ukv),
    ], axis=-1)
    return y @ w_out

def _swiglu(x, w_gate, w_up, w_down):
    return (jax.nn.silu(x @ w_gate) * (x @ w_up)) @ w_down

def _route(xf, w_router, router_bias):
    t = xf.shape[0]
    per_group = N_EXPERTS // N_EXPERT_GROUPS
    scores = jax.nn.sigmoid((xf @ w_router).astype(jnp.float32))
    sel = scores + router_bias.astype(jnp.float32)
    group_score = lax.top_k(sel.reshape(t, N_EXPERT_GROUPS, per_group), 2)[0].sum(-1)
    top_groups = lax.top_k(group_score, TOPK_GROUPS)[1]
    group_mask = jax.nn.one_hot(top_groups, N_EXPERT_GROUPS).sum(1) > 0
    sel = jnp.where(jnp.repeat(group_mask, per_group, axis=1), sel, -jnp.inf)
    top_idx = lax.top_k(sel, TOP_K)[1]
    top_w = jnp.take_along_axis(scores, top_idx, axis=-1)
    top_w = top_w / jnp.sum(top_w, axis=-1, keepdims=True) * ROUTED_SCALE
    return top_idx, top_w

def _routed_experts(xf, top_idx, top_w, w_gate, w_up, w_down):
    t, d = xf.shape
    n_assign = t * TOP_K
    flat_e = top_idx.reshape(-1)
    order = jnp.argsort(flat_e)
    e_sorted = flat_e[order]
    tok_sorted = (order // TOP_K).astype(jnp.int32)
    w_sorted = top_w.reshape(-1)[order].astype(xf.dtype)
    counts = jnp.bincount(flat_e, length=N_EXPERTS)
    padded = (counts + EXPERT_BLOCK - 1) // EXPERT_BLOCK * EXPERT_BLOCK
    pad_end = jnp.cumsum(padded)
    pad_start = pad_end - padded
    start = jnp.cumsum(counts) - counts
    dest = pad_start[e_sorted] + jnp.arange(n_assign) - start[e_sorted]
    n_blocks = -(-(n_assign + N_EXPERTS * (EXPERT_BLOCK - 1)) // EXPERT_BLOCK)
    n_rows = n_blocks * EXPERT_BLOCK
    row_tok = jnp.full((n_rows,), t, jnp.int32).at[dest].set(tok_sorted)
    row_w = jnp.zeros((n_rows,), xf.dtype).at[dest].set(w_sorted)
    block_e = jnp.minimum(
        jnp.searchsorted(pad_end, jnp.arange(n_blocks) * EXPERT_BLOCK, side='right'),
        N_EXPERTS - 1)
    x_rows = jnp.concatenate([xf, jnp.zeros((1, d), xf.dtype)], axis=0)[row_tok]
    x_rows = x_rows.reshape(n_blocks, EXPERT_BLOCK, d)

    def expert_block(args):
        xb, e = args
        return _swiglu(xb, w_gate[e], w_up[e], w_down[e])

    y_rows = lax.map(expert_block, (x_rows, block_e)).reshape(n_rows, d)
    return jax.ops.segment_sum(y_rows * row_w[:, None], row_tok, num_segments=t + 1)[:t]

def _moe(h, w_router, router_bias, w_gate, w_up, w_down, ws_gate, ws_up, ws_down):
    b, s, d = h.shape
    xf = h.reshape(b * s, d)
    top_idx, top_w = _route(xf, w_router, router_bias)
    y = _routed_experts(xf, top_idx, top_w, w_gate, w_up, w_down) + _swiglu(xf, ws_gate, ws_up, ws_down)
    return y.reshape(b, s, d)

def setup_inputs(seed: int = 0) -> dict:
    key = jax.random.key(seed)
    ks = jax.random.split(key, 26)
    L = DEPTH
    f32 = jnp.float32

    def nrm(k, shape, fan_in, mult=1.0):
        return jax.random.normal(k, shape, f32) * (mult * fan_in ** -0.5)

    def gain(k, shape):
        return 1.0 + 0.02 * jax.random.normal(k, shape, f32)

    offsets = jax.random.randint(ks[2], (BATCH, 1), 0, MAX_POS_OFFSET, dtype=jnp.int32)
    positions = offsets + jnp.arange(SEQ, dtype=jnp.int32)[None, :]
    return {
        'x': jax.random.normal(ks[0], (BATCH, SEQ, D_MODEL), f32),
        'c': jax.random.normal(ks[1], (BATCH, D_MODEL), f32),
        'positions': positions,
        'w_ada': nrm(ks[3], (L, D_MODEL, 6 * D_MODEL), D_MODEL, 0.5),
        'b_ada': 0.02 * jax.random.normal(ks[4], (L, 6 * D_MODEL), f32),
        'w_in': nrm(ks[5], (L, D_MODEL, N_IN), D_MODEL),
        'w_pool': nrm(ks[6], (L, POOL_GROUPS, POOL_CH, POOL_CH), POOL_CH),
        'pool_scale': gain(ks[7], (L, POOL_WIDTH)),
        'w_spatial': nrm(ks[8], (L, SG_HEADS, SG_CHUNK, SG_CHUNK), SG_CHUNK),
        'b_spatial': gain(ks[9], (L, SG_HEADS, SG_CHUNK)),
        'g_q': gain(ks[10], (L, Q_LORA)),
        'w_uq': nrm(ks[11], (L, Q_LORA, MLA_HEADS * (QK_NOPE + QK_ROPE)), Q_LORA),
        'g_kv': gain(ks[12], (L, KV_LORA)),
        'w_ukv': nrm(ks[13], (L, KV_LORA, MLA_HEADS * (QK_NOPE + V_DIM)), KV_LORA),
        'w_out': nrm(ks[14], (L, D_MIX, D_MODEL), D_MIX),
        'w_router': nrm(ks[15], (L, D_MODEL, N_EXPERTS), D_MODEL),
        'router_bias': 0.01 * jax.random.normal(ks[16], (L, N_EXPERTS), f32),
        'w_gate': nrm(ks[17], (L, N_EXPERTS, D_MODEL, EXPERT_FF), D_MODEL),
        'w_up': nrm(ks[18], (L, N_EXPERTS, D_MODEL, EXPERT_FF), D_MODEL),
        'w_down': nrm(ks[19], (L, N_EXPERTS, EXPERT_FF, D_MODEL), EXPERT_FF),
        'ws_gate': nrm(ks[20], (L, D_MODEL, SHARED_FF), D_MODEL),
        'ws_up': nrm(ks[21], (L, D_MODEL, SHARED_FF), D_MODEL),
        'ws_down': nrm(ks[22], (L, SHARED_FF, D_MODEL), SHARED_FF),
        'final_gain': gain(ks[23], (D_MODEL,)),
    }

def reference(x, c, positions, w_ada, b_ada, w_in, w_pool, pool_scale, w_spatial, b_spatial,
              g_q, w_uq, g_kv, w_ukv, w_out, w_router, router_bias, w_gate, w_up, w_down,
              ws_gate, ws_up, ws_down, final_gain):
    cond = jax.nn.silu(c)
    for l in range(DEPTH):
        mod = (cond @ w_ada[l] + b_ada[l])[:, None, :]
        shift1, scale1, gate1, shift2, scale2, gate2 = jnp.split(mod, 6, axis=-1)
        h = _ada_norm(x, shift1, scale1)
        x = x + gate1 * _token_mixer(h, positions, w_in[l], w_pool[l], pool_scale[l],
                                     w_spatial[l], b_spatial[l], g_q[l], w_uq[l],
                                     g_kv[l], w_ukv[l], w_out[l])
        h = _ada_norm(x, shift2, scale2)
        x = x + gate2 * _moe(h, w_router[l], router_bias[l], w_gate[l], w_up[l], w_down[l],
                             ws_gate[l], ws_up[l], ws_down[l])
    return _rms_norm(x, final_gain)


_drawn_inputs = setup_inputs


def setup_inputs(seed=0):
    import zlib

    import numpy as np

    out = dict(_drawn_inputs(seed))
    spreads = {}
    factors = {'b_spatial': 2.807, 'g_q': 7.034, 'g_kv': 3.618, 'final_gain': 2.908}
    for name, (base, spread) in spreads.items():
        noise = np.random.default_rng([zlib.crc32(name.encode()), seed]).standard_normal(out[name].shape)
        drawn = base * np.exp(spread * noise) if base else spread * noise
        out[name] = __import__('jax').numpy.asarray(drawn.astype(out[name].dtype))
    for name, factor in factors.items():
        out[name] = (out[name] * factor).astype(out[name].dtype)
    return out
```

```python
from contextlib import ExitStack

import numpy as np

import concourse.bass as bass
from concourse import mybir

ALU = mybir.AluOpType
ACT = mybir.ActivationFunctionType
AX = mybir.AxisListType.X
F32 = mybir.dt.float32
F32R = mybir.dt.float32r
BF16 = mybir.dt.bfloat16
I32 = mybir.dt.int32
U32 = mybir.dt.uint32

P = 128
D = 1024
DC = D // P
T = 512
TJ = T // P
DEPTH = 2
WINDOWS = (2, 4, 8, 16)
GROUP = 64
HEADS, NOPE, ROPE, VDIM = 8, 64, 32, 64
QK = NOPE + ROPE
SCALE = QK ** -0.5
SGH = 4
NIN = 1184
COL_A, COL_U, COL_V, COL_CQ, COL_CKV, COL_PE = 0, 256, 512, 768, 1024, 1152
QL = 256
E, TOPK, NG, PER_G, TOPG = 64, 8, 8, 8, 4
FF = 256
EPS = 1e-6
MAX_BLOCKS = T * TOPK // P + E * (P - 1) // P
MAX_PAIRS = (MAX_BLOCKS + 1) // 2
MIN_PAIRS = T * TOPK // P // 2
LEAST = 4
NTAB = 2 * MAX_PAIRS + 2
NO_SLOT = 65536.0
MASKED = -1.0e30
TAKEN = -2.0e30
PI = float(np.pi)

CONST = {}


def lay_constants():
    parts, at = [], 0

    def put(name, a):
        nonlocal at
        a = np.asarray(a, np.float32).reshape(a.shape[0], -1)
        full = np.zeros((P, a.shape[1]), np.float32)
        full[: a.shape[0]] = a
        CONST[name] = (at, a.shape[1])
        parts.append(full)
        at += a.shape[1]

    k, t = np.arange(P)[:, None], np.arange(P)[None, :]
    put("ident", np.eye(P))
    put("ones", np.ones((P, P)))
    put("before", k < t)
    put("upto", k <= t)
    put("causal", np.where(t <= k, 0.0, MASKED))
    band = np.zeros((P, 4, 3, P))
    for g, w in enumerate(WINDOWS):
        inside = (k <= t) & (k > t - w)
        band[:, g, 0] = inside / np.minimum(t + 1, w) - (k == t)
        band[:, g, 1] = inside / w - (k == t)
        band[:, g, 2] = (k - P > t - w) / w
    put("band", band)
    put("slots", np.broadcast_to(t, (P, P)))
    put("lower_group", np.broadcast_to(np.arange(8)[None, :] < np.arange(8)[:, None], (P, 8, 8)))
    put("token", k + P * np.arange(TJ)[None, :] - NO_SLOT)
    put("block", np.broadcast_to(np.arange(NTAB), (P, NTAB)))
    put("even", np.broadcast_to(2 * np.arange(MAX_PAIRS + 1), (P, MAX_PAIRS + 1)))
    put("steps", np.broadcast_to(P * np.arange(TJ), (P, TJ)))
    freq = (10000.0 ** (-np.arange(0, ROPE, 2, dtype=np.float64) / ROPE)).astype(np.float32)
    put("freq", np.concatenate([np.zeros(NOPE), freq, freq, np.zeros(P - QK)])[:, None])
    put("eps", np.full((P, 1), EPS))
    put("zero", np.zeros((P, 1)))
    return np.concatenate(parts, axis=1)


lay_constants()
NCONST = sum(n for _, n in CONST.values())


def wait(eng, sem, value):
    if isinstance(value, int) and value <= 0:
        return
    eng.wait_ge(sem, value)


def later(s, n):
    return not isinstance(s.n, int) or s.n >= n


class Step:

    def __init__(self, half, par):
        self.half, self.par = half, par
        self.n = half * 2 + par

    def __add__(self, k):
        return Step(self.half + (self.par + k) // 2, (self.par + k) % 2)


def trunk(nc, ins, out, scratch):
    x_in, c_in, positions = ins["x"], ins["c"], ins["positions"]
    h2_dram, y_dram = scratch
    stack = ExitStack()
    with stack:
        def sb_in(where, name, shape, dt=F32):
            return where.enter_context(nc.sbuf_tensor(name, shape, dt))

        def sb(name, shape, dt=F32):
            return sb_in(stack, name, shape, dt)

        def sem(name):
            return stack.enter_context(nc.semaphore(name))

        const = sb("const", [P, NCONST])

        def cst(name, rows=P):
            at, n = CONST[name]
            return const[0:rows, at:at + n]

        ident, ones = cst("ident"), cst("ones")
        x = sb("x", [P, TJ, D])
        mod = sb("mod", [P, 6, D])
        rotary = sb("rotary", [P, 2, T])
        cos, sin = rotary[:, 0, :], rotary[:, 1, :]
        h = sb("h", [P, 2, D])
        hT = sb("hT", [P, DC, T])
        mixT = sb("mixT", [P, DC, T])
        stat = sb("stat", [P, 32])
        identb = sb("identb", [P, P], BF16)
        causalb = sb("causalb", [P, P], BF16)
        SHIFT1, SCALE1, GATE1, SHIFT2, SCALE2, GATE2 = range(6)
        bank = [stack.enter_context(nc.psum_tensor(f"bank{i}", [P, 512], F32)) for i in range(8)]

        def dram(name, l):
            return ins[name][bass.ds(l, 1)]

        gathered_dma = [sem(f"gathered_dma{i}") for i in range(2)]
        scattered_dma = [sem(f"scattered_dma{i}") for i in range(2)]
        s_start = sem("s_start")
        s_final_load, s_final, s_out = sem("s_final_load"), sem("s_final"), sem("s_out")

        start_block = nc.Block()
        with start_block as block:
            @block.sync
            def _(sp):
                sp.dma_start(const[:], ins["const"]).then_inc(s_start, 16)
                sp.dma_start(x[:], x_in.rearrange("o (j p) n -> p (o j) n", p=P)).then_inc(s_start, 16)
                sp.dma_start(hT[:, 0, :].bitcast(I32), positions.to_broadcast([P, T])).then_inc(s_start, 16)

            @block.vector
            def _(dve):
                done = [48]

                def link(i):
                    done[0] += 1
                    i.then_inc(s_start, 1)
                    dve.wait_ge(s_start, done[0])

                dve.wait_ge(s_start, 48)
                link(dve.tensor_copy(identb[:], ident))
                link(dve.tensor_copy(causalb[:], cst("causal")))
                ang, turns, red = hT[:, 1, :], hT[:, 2, :], hT[:, 3, :]
                link(dve.tensor_copy(red, hT[:, 0, :].bitcast(I32)))
                link(dve.tensor_scalar(ang, red, cst("freq"), None, ALU.mult))
                MAGIC = 1.5 * 2.0 ** 23
                TURN1, TURN2 = 6.28125, float(np.float32(2 * np.pi - 6.28125))
                for shift, to in ((0.0, sin), (0.25, cos)):
                    link(dve.tensor_scalar(turns, ang, 1.0 / (2 * PI), shift, ALU.mult, ALU.add))
                    link(dve.tensor_scalar(turns, turns, MAGIC, None, ALU.add))
                    link(dve.tensor_scalar(turns, turns, -MAGIC, None, ALU.add))
                    link(dve.scalar_tensor_tensor(out=red, in0=turns, scalar=-TURN1, in1=ang, op0=ALU.mult, op1=ALU.add))
                    link(dve.scalar_tensor_tensor(out=red, in0=turns, scalar=-TURN2, in1=red, op0=ALU.mult, op1=ALU.add))
                    link(dve.tensor_scalar(red, red, shift * 2 * PI, None, ALU.add))
                    link(dve.tensor_scalar(to, red, PI, -PI, ALU.min, ALU.max))

            @block.scalar
            def _(act):
                act.wait_ge(s_start, 48 + 4 + 14)
                act.activation(sin, sin, ACT.Sin).then_inc(s_start, 1)
                act.activation(cos, cos, ACT.Sin).then_inc(s_start, 1)
                act.wait_ge(s_start, 48 + 4 + 16)

        cum_pairs = nc.gpsimd.alloc_register("cum_pairs")
        nc.gpsimd.reg_mov(cum_pairs, 0)

        layers = stack.enter_context(ExitStack())
        l = layers.enter_context(nc.Fori(0, DEPTH))
        mixer(nc, ins, l, locals())
        experts(nc, ins, l, locals())
        layers.close()

        with nc.Block() as block:
            gain = mod[:, 0, :]

            @block.sync
            def _(sp):
                sp.dma_start(gain, ins["final_gain"].rearrange("(o n) -> o n", o=1).to_broadcast([P, D])).then_inc(s_final_load, 16)
                for j in range(TJ):
                    sp.wait_ge(s_final, 11 + j)
                    sp.dma_start(out.rearrange("o (j p) n -> p (o j) n", p=P)[:, j, :], x[:, j, :]).then_inc(s_out, 16)
                sp.wait_ge(s_out, 16 * TJ)

            @block.scalar
            def _(act):
                for j in range(TJ):
                    act.activation(hT[:, 2 * j:2 * j + 2, :].rearrange("p a n -> p (a n)"), x[:, j, :], ACT.Square,
                                   accum_out=stat[:, j:j + 1]).then_inc(s_final, 1)
                act.wait_ge(s_final, TJ)
                act.activation(stat[:, 4:8], stat[:, 0:4], ACT.Sqrt, bias=cst("eps"), scale=1.0 / D).then_inc(s_final, 1)

            @block.vector
            def _(dve):
                dve.wait_ge(s_final, 5)
                dve.reciprocal(stat[:, 8:12], stat[:, 4:8]).then_inc(s_final, 5)
                dve.wait_ge(s_final, 10)
                dve.wait_ge(s_final_load, 16)
                for j in range(TJ):
                    dve.scalar_tensor_tensor(out=x[:, j, :], in0=x[:, j, :], scalar=stat[:, 8 + j:9 + j], in1=gain,
                                             op0=ALU.mult, op1=ALU.mult).then_inc(s_final, 1)


def clear(nc, sems):
    nums = [s.num for s in sems]
    assert max(nums) - min(nums) + 1 == len(nums)
    nc.all_engine_barrier(sems_to_clear=range(min(nums), max(nums) + 1))


def mixer(nc, ins, l, v):
    const, cst, x, mod, cos, sin, h, hT, mixT, stat, bank, dram = (
        v[k] for k in "const cst x mod cos sin h hT mixT stat bank dram".split())
    ident, ones, identb, causalb = v["ident"], v["ones"], v["identb"], v["causalb"]
    SHIFT1, SCALE1, GATE1 = 0, 1, 2
    with ExitStack() as stack:
        def sb(name, shape, dt=F32):
            return stack.enter_context(nc.sbuf_tensor(name, shape, dt))

        sems = []

        def sem(name):
            sems.append(stack.enter_context(nc.semaphore(name)))
            return sems[-1]

        w_in = sb("w_in_sb", [P, DC, NIN])
        w_out = w_in[:].rearrange("p a b -> p (a b)")[:, 0:DC * D].rearrange("p (m n) -> p m n", m=DC)
        w_uq = sb("w_uq_sb", [P, 2, HEADS, QK])
        w_uq_rot = sb("w_uq_rot", [P, 2, HEADS, QK])
        w_k_rot = sb("w_k_rot", [P, DC, QK])
        w_ukv = sb("w_ukv_sb", [P, HEADS, NOPE + VDIM])
        w_sp = sb("w_sp", [P, SGH, P])
        w_spT = sb("w_spT", [P, SGH, P])
        b_sp = sb("b_sp", [1, SGH, P])
        w_pool = sb("w_pool_sb", [P, 2, P])
        pool_scale = sb("pool_scale_sb", [P, 2])
        g_q, g_kv = sb("g_q_sb", [P, 2]), sb("g_kv_sb", [P, 1])
        cond = sb("cond", [P, 2, DC])
        a_sb, v_sb = sb("a_sb", [P, TJ, 256]), sb("v_sb", [P, TJ, 256])
        latent = sb("latent", [P, 3, T])
        q_sb, k_sb = sb("q_sb", [QK, 2, T]), sb("k_sb", [QK, 2, T])
        k_pe = mixT[:, 0:2, :]
        tmp = sb("tmp", [P, 2, T])
        b_row = v["rotary"][0:1, :, :]
        acc = sb("acc", [P, 2, 512])
        w_ada = sb("w_ada_sb", [P, 2, DC // 2, 512])
        rs = sb("rs", [P, 4 * HEADS * TJ])
        bn = sb("bn", [P, TJ, 8])
        v_att = hT[:, 0:4, :].rearrange("p j (h d) -> p j h d", h=HEADS)
        o_att = hT[:, 4:8, :]
        probs = h[:, :, 0:512]
        probsT = h[:, :, 512:1024]
        dT = tmp

        d_small, d_in, d_mid, d_out = sem("d_small"), sem("d_in"), sem("d_mid"), sem("d_out")
        d_ada = [sem("d_ada0"), sem("d_ada1")]
        d_row = [sem("d_row0"), sem("d_row1")]
        s_cond, s_ms, s_rms, s_link, s_alink = sem("s_cond"), sem("s_ms"), sem("s_rms"), sem("s_link"), sem("s_alink")
        s_unit, s_acc, s_modps, s_mod = sem("s_unit"), sem("s_acc"), sem("s_modps"), sem("s_mod")
        s_h, s_hTps, s_hT = sem("s_h"), sem("s_hTps"), sem("s_hT")
        s_rot, s_av, s_ave, s_vg = sem("s_rot"), sem("s_av"), sem("s_ave"), sem("s_vg")
        s_proj, s_pe, s_u, s_lat = sem("s_proj"), sem("s_pe"), sem("s_u"), sem("s_lat")
        s_sq, s_ssq, s_root, s_norm = sem("s_sq"), sem("s_ssq"), sem("s_root"), sem("s_norm")
        s_vn, s_wsT, s_wsTe, s_mixed, s_sg = sem("s_vn"), sem("s_wsT"), sem("s_wsTe"), sem("s_mixed"), sem("s_sg")
        s_dT, s_dTe, s_yT, s_yTe = sem("s_dT"), sem("s_dTe"), sem("s_yT"), sem("s_yTe")
        s_vatt, s_vatte = sem("s_vatt"), sem("s_vatte")
        s_qk, s_k, s_qn, s_q, s_kpe = sem("s_qk"), sem("s_k"), sem("s_qn"), sem("s_q"), sem("s_kpe")
        s_oe, s_S, s_max, s_exp, s_PT, s_PTe, s_O = sem("s_oe"), sem("s_S"), sem("s_max"), sem("s_exp"), sem("s_PT"), sem("s_PTe"), sem("s_O")
        s_o, s_oT, s_oTe, s_y, s_x, s_wp0 = sem("s_o"), sem("s_oT"), sem("s_oTe"), sem("s_y"), sem("s_x"), sem("s_wp0")

        ada_src = dram("w_ada", l).rearrange("o (p c) n -> p (o c) n", c=DC)
        N_SOFT = HEADS * TJ

        with nc.Block() as block:
            @block.sync
            def _(sp):
                def ada(u):
                    q, half = u // 2, u % 2
                    wait(sp, s_unit, u - 1)
                    sp.dma_start(w_ada[:, u % 2], ada_src[:, half * 4:half * 4 + 4, q * 512:q * 512 + 512]).then_inc(d_ada[u % 2], 16)
                    if half == 0:
                        wait(sp, s_modps, q - 1)
                        sp.dma_start(b_row[:, q % 2, :], dram("b_ada", l)[:, q * 512:q * 512 + 512]).then_inc(d_row[q % 2], 16)

                sp.dma_start(cond[:, 0, :], ins["c"].rearrange("o (p c) -> p (o c)", c=DC)).then_inc(d_small, 16)
                ada(0)
                ada(1)
                sp.dma_start(w_in[:], dram("w_in", l).rearrange("o (p c) n -> p (o c) n", c=DC)).then_inc(d_in, 16)
                for u in range(2, 8):
                    ada(u)
                sp.dma_start(w_uq[:].rearrange("p m h q -> p m (h q)"), dram("w_uq", l).rearrange("o (m p) n -> p (o m) n", p=P)).then_inc(d_mid, 16)
                sp.dma_start(w_ukv[:].rearrange("p h q -> p (h q)"), dram("w_ukv", l).rearrange("o p n -> p (o n)")).then_inc(d_mid, 16)
                sp.dma_start(w_sp[:], dram("w_spatial", l).rearrange("o h t k -> t (o h) k")).then_inc(d_mid, 16)
                sp.dma_start(b_sp[:], dram("b_spatial", l)).then_inc(d_mid, 16)
                with nc.allow_non_contiguous_dma(reason="short vectors, a feature to a partition"):
                    sp.dma_start(pool_scale[:], dram("pool_scale", l).rearrange("o (m p) -> p (o m)", p=P)).then_inc(d_mid, 16)
                    sp.dma_start(g_q[:], dram("g_q", l).rearrange("o (m p) -> p (o m)", p=P)).then_inc(d_mid, 16)
                    sp.dma_start(g_kv[:], dram("g_kv", l).rearrange("o p -> p o")).then_inc(d_mid, 16)
                sp.wait_ge(s_wp0, 1)
                for g in range(2):
                    sp.dma_start(w_pool[64 * g:64 * g + 64, :, 64 * g:64 * g + 64],
                                 dram("w_pool", l).rearrange("o (m g) c d -> g c (o m) d", g=2)[g]).then_inc(d_mid, 16)
                for u in range(8, 16):
                    ada(u)
                sp.wait_ge(s_proj, 7)
                sp.wait_ge(s_av, TJ)
                sp.dma_start(w_out, dram("w_out", l).rearrange("o (m p) n -> p (o m) n", p=P)).then_inc(d_out, 16)
                for u in range(16, 24):
                    ada(u)

            @block.gpsimd
            def _(pool):
                pool.memset(w_pool[:], 0.0).then_inc(s_wp0, 1)
                pool.memset(w_k_rot[:, :, 0:NOPE], 0.0)
                pool.memset(w_uq_rot[:, :, :, 0:NOPE], 0.0)
                half = ROPE // 2
                pool.wait_ge(d_in, 16)
                pool.tensor_scalar(w_k_rot[:, :, NOPE:NOPE + half], w_in[:, :, COL_PE + half:COL_PE + ROPE], -1.0, 0.0, ALU.mult, ALU.add)
                pool.tensor_copy(w_k_rot[:, :, NOPE + half:QK], w_in[:, :, COL_PE:COL_PE + half]).then_inc(s_rot, 1)
                pool.wait_ge(d_mid, 16 * 9)
                for m in range(2):
                    pool.tensor_scalar(w_uq_rot[:, m, :, NOPE:NOPE + half], w_uq[:, m, :, NOPE + half:QK], -1.0, 0.0, ALU.mult, ALU.add)
                    i = pool.tensor_copy(w_uq_rot[:, m, :, NOPE + half:QK], w_uq[:, m, :, NOPE:NOPE + half])
                i.then_inc(s_rot, 1)

            @block.scalar
            def _(act):
                act.wait_ge(d_small, 16)
                act.activation(cond[:, 1, :], cond[:, 0, :], ACT.Silu).then_inc(s_cond, 1)
                for j in range(TJ):
                    act.activation(mixT[:, 2 * j:2 * j + 2, :].rearrange("p a n -> p (a n)"), x[:, j, :], ACT.Square,
                                   accum_out=stat[:, j:j + 1]).then_inc(s_ms, 1)
                act.wait_ge(s_ms, TJ)
                act.activation(stat[:, 4:8], stat[:, 0:4], ACT.Sqrt, bias=cst("eps"), scale=1.0 / D).then_inc(s_rms, 1)

                def mod_out(q):
                    act.wait_ge(s_modps, q + 1)
                    bias = 1.0 if q // 2 in (SCALE1, 4) else 0.0
                    act.activation(mod[:, q // 2, (q % 2) * 512:(q % 2) * 512 + 512], bank[7][:], ACT.Copy, bias=bias).then_inc(s_mod, 1)

                for q in range(4):
                    mod_out(q)
                for j in range(TJ):
                    act.wait_ge(s_hTps, j + 1)
                    for b in range(2):
                        i = act.activation(hT[:, 4 * b:4 * b + 4, j * P:j * P + P],
                                           bank[2 * (j % 2) + b][:].rearrange("p (c t) -> p c t", c=4), ACT.Copy)
                    i.then_inc(s_hT, 1)
                for j in range(TJ):
                    act.wait_ge(s_ave, j + 1)
                    act.activation(v_sb[:, j, :], bank[4 + j % 2][:, 256:512], ACT.Gelu_apprx_tanh).then_inc(s_vg, 1)
                for m in range(2):
                    act.wait_ge(s_proj, m + 1)
                    act.activation(mixT[:, 2 + m, :], bank[m][:], ACT.Gelu_apprx_tanh).then_inc(s_u, 1)
                for n in range(2):
                    act.wait_ge(s_ssq, n + 1)
                    act.activation(tmp[:, n, :], bank[4 + n][:], ACT.Sqrt, bias=cst("eps"), scale=1.0 / (QL if n == 0 else P)).then_inc(s_root, 1)
                for j in range(TJ):
                    act.wait_ge(s_vn, j + 1)
                    act.activation(bn[:, j, 3:4], bn[:, j, 1:2], ACT.Sqrt, bias=cst("eps")).then_inc(s_root, 1)
                for j in range(TJ):
                    act.wait_ge(s_vatt, j + 1)
                    act.activation(hT[:, j, :], bank[4 + j % 2][:], ACT.Copy).then_inc(s_vatte, 1)
                for m in range(2):
                    act.wait_ge(s_yT, m + 1)
                    act.mul(mixT[:, m, :], bank[2 + m][:], pool_scale[:, m:m + 1]).then_inc(s_yTe, 1)

                def head_out(hd):
                    act.wait_ge(s_qk, hd + 1)
                    if hd >= 2:
                        act.wait_ge(s_S, (hd - 1) * TJ)
                    act.activation(q_sb[0:NOPE, hd % 2, :], bank[0][0:NOPE, :], ACT.Copy).then_inc(s_qn, 1)
                    act.activation(k_sb[0:NOPE, hd % 2, :], bank[2][0:NOPE, :], ACT.Copy).then_inc(s_k, 1)

                head_out(0)
                n = 0
                for hd in range(HEADS):
                    for i in range(TJ):
                        act.wait_ge(s_max, n + 1)
                        if n >= 2:
                            act.wait_ge(s_PT, n - 1)
                        act.activation(probs[:, n % 2, 0:(i + 1) * P], bank[3 + n % 2][:, 0:(i + 1) * P], ACT.Exp,
                                       scale=SCALE, bias=rs[:, N_SOFT + n:N_SOFT + n + 1],
                                       accum_out=rs[:, 2 * N_SOFT + n:2 * N_SOFT + n + 1]).then_inc(s_exp, 1)
                        n += 1
                        if i == 2 and hd + 1 < HEADS:
                            head_out(hd + 1)
                        if i == 3 and hd >= 1:
                            mod_out(3 + hd)
                mod_out(11)
                for i in range(TJ):
                    act.wait_ge(s_oT, i + 1)
                    act.activation(mixT[:, 4:8, i * P:i * P + P], bank[5][:].rearrange("p (m t) -> p m t", m=4), ACT.Copy).then_inc(s_oTe, 1)
                for j in range(TJ):
                    act.wait_ge(s_x, 2 * j + 2)
                    act.activation(h[:, 0, :], x[:, j, :], ACT.Square, accum_out=stat[:, 16 + j:17 + j]).then_inc(s_alink, 1)
                    act.wait_ge(s_alink, j + 1)
                act.activation(stat[:, 20:24], stat[:, 16:20], ACT.Sqrt, bias=cst("eps"), scale=1.0 / D).then_inc(s_alink, 1)

            @block.vector
            def _(dve):
                links = [0]

                def link(i):
                    links[0] += 1
                    i.then_inc(s_link, 1)
                    dve.wait_ge(s_link, links[0])

                def ada(q, some=range(DC)):
                    for k in some:
                        u, c = 2 * q + k // 4, k % 4
                        if k == 0:
                            if q < 1:
                                dve.wait_ge(s_cond, 1)
                            wait(dve, s_modps, q - 1)
                        if c == 0:
                            dve.wait_ge(d_ada[u % 2], 16 * (u // 2 + 1))
                        w, by = w_ada[:, u % 2, c, :], cond[:, 1, k:k + 1]
                        if k == 0:
                            i = dve.tensor_scalar(acc[:, q % 2, :], w, by, None, ALU.mult)
                        else:
                            i = dve.scalar_tensor_tensor(out=acc[:, q % 2, :], in0=w, scalar=by, in1=acc[:, q % 2, :], op0=ALU.mult, op1=ALU.add)
                        if c < 3:
                            link(i)
                        else:
                            i.then_inc(s_unit, 1)
                            dve.wait_ge(s_unit, u + 1)

                def pt(n):
                    hd, i = n // TJ, n % TJ
                    dve.wait_ge(s_PT, n + 1)
                    if n >= 2:
                        dve.wait_ge(s_O, n - 1)
                    dve.tensor_copy(probsT[:, n % 2, 0:(i + 1) * P], bank[5][:, 0:(i + 1) * P]).then_inc(s_PTe, 1)
                    if i == 0 and hd >= 1:
                        o_out(hd - 1)

                def o_out(hd):
                    dve.wait_ge(s_O, (hd + 1) * TJ)
                    dve.tensor_copy(o_att.rearrange("p i (h d) -> p i h d", d=VDIM)[:, :, hd, :],
                                    bank[6][:, 0:256].rearrange("p (i d) -> p i d", i=TJ)).then_inc(s_oe, 1)

                for q in range(4):
                    ada(q)
                dve.wait_ge(s_rms, 1)
                link(dve.reciprocal(stat[:, 8:12], stat[:, 4:8]))
                dve.wait_ge(s_mod, 4)
                for j in range(TJ):
                    wait(dve, s_hTps, j - 1)
                    link(dve.scalar_tensor_tensor(out=h[:, j % 2, :], in0=x[:, j, :], scalar=stat[:, 8 + j:9 + j], in1=mod[:, SCALE1, :], op0=ALU.mult, op1=ALU.mult))
                    dve.tensor_tensor(h[:, j % 2, :], h[:, j % 2, :], mod[:, SHIFT1, :], ALU.add).then_inc(s_h, 1)
                for j in range(TJ):
                    dve.wait_ge(s_av, j + 1)
                    dve.tensor_copy(a_sb[:, j, :], bank[4 + j % 2][:, 0:256]).then_inc(s_ave, 1)
                for m in range(3):
                    dve.wait_ge(s_proj, 3 + m)
                    link(dve.tensor_copy(latent[:, m, :], bank[(2, 3, 6)[m]][:]))
                    dve.tensor_tensor(mixT[:, 4 + m, :], latent[:, m, :], latent[:, m, :], ALU.mult).then_inc(s_sq, 1)
                dve.wait_ge(s_proj, 7)
                R = slice(NOPE, QK)
                link(dve.tensor_tensor(k_pe[R, 0, :], bank[0][R, :], cos[R, :], ALU.mult))
                link(dve.tensor_tensor(k_pe[R, 1, :], bank[1][R, :], sin[R, :], ALU.mult))
                for b in range(2):
                    i = dve.tensor_tensor(k_sb[R, b, :], k_pe[R, 0, :], k_pe[R, 1, :], ALU.add)
                i.then_inc(s_kpe, 1)
                for j in range(TJ):
                    dve.wait_ge(s_vg, j + 1)
                    link(dve.bn_stats(rs[:, 8 * j:8 * j + 6], v_sb[:, j, :]))
                    dve.bn_aggr(bn[:, j, 0:2], rs[:, 8 * j:8 * j + 6]).then_inc(s_vn, 1)
                for n in range(2):
                    dve.wait_ge(s_root, n + 1)
                    link(dve.reciprocal(tmp[:, n, :], tmp[:, n, :]))
                dve.wait_ge(d_mid, 16 * 9)
                for m in range(3):
                    g = g_q[:, m:m + 1] if m < 2 else g_kv[:, 0:1]
                    i = dve.scalar_tensor_tensor(out=latent[:, m, :], in0=latent[:, m, :], scalar=g, in1=tmp[:, m // 2, :], op0=ALU.mult, op1=ALU.mult)
                i.then_inc(s_norm, 1)
                for j in range(TJ):
                    dve.wait_ge(s_root, 3 + j)
                    link(dve.reciprocal(bn[:, j, 4:5], bn[:, j, 3:4]))
                    dve.tensor_scalar(v_sb[:, j, :], v_sb[:, j, :], bn[:, j, 0:1], bn[:, j, 4:5], ALU.subtract, ALU.mult).then_inc(s_vn, 1)
                dve.wait_ge(s_wsT, 1)
                dve.tensor_tensor(w_spT[:], bank[6][:].rearrange("p (h t) -> p h t", h=SGH),
                                  cst("upto").unsqueeze(1).to_broadcast([P, SGH, P]), ALU.mult).then_inc(s_wsTe, 1)
                for m in range(2):
                    dve.wait_ge(s_dT, m + 1)
                    dve.tensor_copy(dT[:, m, :], bank[2 + m][:]).then_inc(s_dTe, 1)
                for m in range(2):
                    dve.wait_ge(s_mixed, m + 1)
                    dve.wait_ge(s_u, 2)
                    dve.tensor_tensor(mixT[:, 2 + m, :], mixT[:, 2 + m, :], bank[m][:], ALU.mult).then_inc(s_sg, 1)
                dve.wait_ge(s_yT, 2)

                def rotate(hd):
                    dve.wait_ge(s_qk, hd + 1)
                    if hd >= 2:
                        dve.wait_ge(s_S, (hd - 1) * TJ)
                    link(dve.tensor_tensor(tmp[R, 1, :], bank[1][R, :], sin[R, :], ALU.mult))
                    dve.wait_ge(s_qn, hd + 1)
                    link(dve.tensor_tensor(tmp[R, 0, :], bank[0][R, :], cos[R, :], ALU.mult))
                    dve.tensor_tensor(q_sb[R, hd % 2, :], tmp[R, 0, :], tmp[R, 1, :], ALU.add).then_inc(s_q, 1)

                rotate(0)
                n = 0
                for hd in range(HEADS):
                    for i in range(TJ):
                        dve.wait_ge(s_S, n + 1)
                        link(dve.reduce_max(rs[:, n:n + 1], bank[3 + n % 2][:, 0:(i + 1) * P], AX))
                        dve.tensor_scalar(rs[:, N_SOFT + n:N_SOFT + n + 1], rs[:, n:n + 1], -SCALE, None, ALU.mult).then_inc(s_max, 1)
                        if n >= 1:
                            pt(n - 1)
                        if i == 2 and hd + 1 < HEADS:
                            rotate(hd + 1)
                        ada(4 + hd, range(2 * i, 2 * i + 2))
                        n += 1
                pt(n - 1)
                o_out(HEADS - 1)
                dve.wait_ge(s_exp, N_SOFT)
                link(dve.reciprocal(rs[:, 3 * N_SOFT:4 * N_SOFT], rs[:, 2 * N_SOFT:3 * N_SOFT]))
                dve.wait_ge(s_oe, HEADS)
                sums = rs[:, 3 * N_SOFT:4 * N_SOFT].rearrange("p (h i) -> p h i", i=TJ)
                for i in range(TJ):
                    dst = o_att[:, i, :].rearrange("p (h d) -> p h d", d=VDIM)
                    dve.tensor_tensor(dst, dst, sums[:, :, i].unsqueeze(2).to_broadcast([P, HEADS, VDIM]), ALU.mult).then_inc(s_o, 1)
                dve.wait_ge(s_mod, 6)
                for j in range(TJ):
                    for b in range(2):
                        n = 2 * j + b
                        dve.wait_ge(s_y, n + 1)
                        link(dve.tensor_tensor(tmp[:, b, :], bank[n % 4][:], mod[:, GATE1, b * 512:b * 512 + 512], ALU.mult))
                        dve.tensor_tensor(x[:, j, b * 512:b * 512 + 512], x[:, j, b * 512:b * 512 + 512], tmp[:, b, :], ALU.add).then_inc(s_x, 1)

            @block.tensor
            def _(pe):
                def ada(q):
                    pe.wait_ge(s_unit, 2 * q + 2)
                    pe.wait_ge(d_row[q % 2], 16 * (q // 2 + 1))
                    wait(pe, s_mod, q)
                    pe.matmul(bank[7][:], ones, acc[:, q % 2, :], start=True, stop=False)
                    pe.matmul(bank[7][:], ones[0:1, :], b_row[:, q % 2, :], start=False, stop=True).then_inc(s_modps, 1)

                for q in range(4):
                    ada(q)
                for j in range(TJ):
                    pe.wait_ge(s_h, j + 1)
                    wait(pe, s_hT, j - 1)
                    for c in range(DC):
                        i = pe.transpose(bank[2 * (j % 2) + c // 4][:, (c % 4) * P:(c % 4) * P + P], h[:, j % 2, c:D:DC], ident)
                    i.then_inc(s_hTps, 1)
                pe.wait_ge(d_in, 16)
                for j in range(TJ):
                    pe.wait_ge(s_hT, j + 1)
                    if j >= 2:
                        pe.wait_ge(s_ave, j - 1)
                        pe.wait_ge(s_vg, j - 1)
                    for c in range(DC):
                        i = pe.matmul(bank[4 + j % 2][:], hT[:, c, j * P:j * P + P],
                                      w_in[:, c, 0:1024].rearrange("p (a b) -> p a b", a=2)[:, :, 0:256], start=c == 0, stop=c == DC - 1)
                    i.then_inc(s_av, 1)
                pe.wait_ge(s_rot, 1)
                plan = [(0, w_in, COL_U, P), (1, w_in, COL_U + P, P), (2, w_in, COL_CQ, P), (3, w_in, COL_CQ + P, P),
                        (6, w_in, COL_CKV, P), (0, w_in, COL_PE - NOPE, QK), (1, w_k_rot, 0, QK)]
                for n, (b, w, col, m) in enumerate(plan):
                    if n >= 5:
                        pe.wait_ge(s_u, n - 4)
                    for c in range(DC):
                        i = pe.matmul(bank[b][0:m, :], w[:, c, col:col + m], hT[:, c, :], start=c == 0, stop=c == DC - 1)
                    i.then_inc(s_proj, 1)
                pe.wait_ge(s_sq, 3)
                pe.wait_ge(s_ave, TJ)
                pe.wait_ge(s_vg, TJ)
                pe.matmul(bank[4][:], ones, mixT[:, 4, :], start=True, stop=False)
                pe.matmul(bank[4][:], ones, mixT[:, 5, :], start=False, stop=True).then_inc(s_ssq, 1)
                pe.matmul(bank[5][:], ones, mixT[:, 6, :], start=True, stop=True).then_inc(s_ssq, 1)
                pe.wait_ge(d_mid, 16 * 9)
                for hd in range(SGH):
                    i = pe.transpose(bank[6][:, hd * P:hd * P + P], w_sp[:, hd, :], ident)
                i.then_inc(s_wsT, 1)
                pe.wait_ge(s_sq, 3)
                at = CONST["band"][0]
                for m in range(2):
                    for gg in range(2):
                        g = 2 * m + gg
                        for j in range(TJ):
                            dst = bank[2 + m][64 * gg:64 * gg + 64, j * P:j * P + P]
                            kind = 0 if j == 0 else 1
                            i = pe.matmul(dst, a_sb[:, j, g * 64:g * 64 + 64], const[:, at + (g * 3 + kind) * P:at + (g * 3 + kind + 1) * P],
                                          start=True, stop=j == 0)
                            if j:
                                i = pe.matmul(dst, a_sb[:, j - 1, g * 64:g * 64 + 64], const[:, at + (g * 3 + 2) * P:at + (g * 3 + 3) * P],
                                              start=False, stop=True)
                    i.then_inc(s_dT, 1)
                pe.wait_ge(s_norm, 1)
                for j in range(TJ):
                    pe.wait_ge(s_root, 2)
                    wait(pe, s_vatte, j - 1)
                    pe.matmul(bank[4 + j % 2][:], latent[:, 2, j * P:j * P + P], w_ukv[:, :, NOPE:], start=True, stop=True).then_inc(s_vatt, 1)
                pe.wait_ge(s_vn, 2 * TJ)
                pe.wait_ge(s_wsTe, 1)
                pe.wait_ge(s_kpe, 1)
                for m in range(2):
                    for gg in range(2):
                        hd = 2 * m + gg
                        for j in range(TJ):
                            dst = bank[m][64 * gg:64 * gg + 64, j * P:j * P + P]
                            pe.matmul(dst, v_sb[:, j, hd * 64:hd * 64 + 64], w_spT[:, hd, :], start=True, stop=False)
                            i = pe.matmul(dst, ones[0:1, 0:64], b_sp[:, hd, :], start=False, stop=True)
                    i.then_inc(s_mixed, 1)
                for m in range(2):
                    pe.wait_ge(s_dTe, m + 1)
                    pe.matmul(bank[2 + m][:], w_pool[:, m, :], dT[:, m, :], start=True, stop=True).then_inc(s_yT, 1)

                def project(hd):
                    if hd == 0:
                        pe.wait_ge(s_rot, 2)
                        pe.wait_ge(s_sg, 2)
                        pe.wait_ge(s_yTe, 2)
                        pe.wait_ge(s_vatte, TJ)
                    else:
                        pe.wait_ge(s_q, hd)
                        pe.wait_ge(s_k, hd)
                    for b, w in ((0, w_uq), (1, w_uq_rot)):
                        for m in range(2):
                            pe.matmul(bank[b][0:QK, :], w[:, m, hd, :], latent[:, m, :], start=m == 0, stop=m == 1)
                    pe.matmul(bank[2][0:NOPE, :], w_ukv[:, hd, 0:NOPE], latent[:, 2, :], start=True, stop=True).then_inc(s_qk, 1)

                def scores(n):
                    hd, i = n // TJ, n % TJ
                    pe.wait_ge(s_q, hd + 1)
                    pe.wait_ge(s_k, hd + 1)
                    if n >= 2:
                        pe.wait_ge(s_exp, n - 1)
                    dst = bank[3 + n % 2]
                    pe.matmul(dst[:, 0:(i + 1) * P], q_sb[:, hd % 2, i * P:i * P + P], k_sb[:, hd % 2, 0:(i + 1) * P], start=True, stop=False)
                    pe.matmul(dst[:, i * P:i * P + P], identb[:], causalb[:], start=False, stop=True).then_inc(s_S, 1)

                def turn(n):
                    i = n % TJ
                    pe.wait_ge(s_exp, n + 1)
                    wait(pe, s_PTe, n)
                    for k in range(i + 1):
                        ins_ = pe.transpose(bank[5][:, k * P:k * P + P], probs[:, n % 2, k * P:k * P + P], ident)
                    ins_.then_inc(s_PT, 1)

                def attend(n):
                    hd, i = n // TJ, n % TJ
                    pe.wait_ge(s_PTe, n + 1)
                    if i == 0 and hd >= 1:
                        pe.wait_ge(s_oe, hd)
                    at = i * VDIM
                    for k in range(i + 1):
                        ins_ = pe.matmul(bank[6][:, at:at + VDIM], probsT[:, n % 2, k * P:k * P + P], v_att[:, k, hd, :],
                                         start=k == 0, stop=k == i)
                    ins_.then_inc(s_O, 1)

                project(0)
                scores(0)
                for n in range(N_SOFT):
                    if n + 1 < N_SOFT:
                        scores(n + 1)
                    if n % TJ == 1 and n // TJ + 1 < HEADS:
                        project(n // TJ + 1)
                    turn(n)
                    if n % TJ == 2 and n >= TJ:
                        ada(3 + n // TJ)
                    if n >= 1:
                        attend(n - 1)
                attend(N_SOFT - 1)
                ada(3 + HEADS)
                for i in range(TJ):
                    pe.wait_ge(s_o, i + 1)
                    if i:
                        pe.wait_ge(s_oTe, i)
                    for m in range(4):
                        ins_ = pe.transpose(bank[5][:, m * P:m * P + P], o_att[:, i, m * P:m * P + P], ident)
                    ins_.then_inc(s_oT, 1)
                pe.wait_ge(d_out, 16)
                for j in range(TJ):
                    pe.wait_ge(s_oTe, j + 1)
                    for b in range(2):
                        n = 2 * j + b
                        wait(pe, s_x, n - 3)
                        for m in range(DC):
                            i = pe.matmul(bank[n % 4][:], mixT[:, m, j * P:j * P + P], w_out[:, m, b * 512:b * 512 + 512], start=m == 0, stop=m == DC - 1)
                        i.then_inc(s_y, 1)
        clear(nc, sems)


def experts(nc, ins, l, v):
    cst, x, mod, h, hT, mixT, stat, bank, dram = (v[k] for k in "cst x mod h hT mixT stat bank dram".split())
    ident, ones, cum_pairs = v["ident"], v["ones"], v["cum_pairs"]
    h2_dram, y_dram, gathered_dma, scattered_dma = v["h2_dram"], v["y_dram"], v["gathered_dma"], v["scattered_dma"]
    SHIFT2, SCALE2, GATE2 = 3, 4, 5
    with ExitStack() as stack:
        def sb(name, shape, dt=F32):
            return stack.enter_context(nc.sbuf_tensor(name, shape, dt))

        sems = []

        def sem(name):
            sems.append(stack.enter_context(nc.semaphore(name)))
            return sems[-1]

        raw_gu = [sb(f"raw_gu{i}", [P, 2, DC, FF]) for i in range(2)]
        raw_d = [sb(f"raw_d{i}", [P, 2, D]) for i in range(2)]
        meta = sb("meta", [P, TJ, E, 3])
        rank = sb("rank", [P, E, TJ])
        listed = sb("listed", [P, NTAB, 3])
        rank_off = sb("rank_off", [P, NTAB])
        block_expert = sb("block_expert", [1, NTAB], I32)
        block_rows = sb("block_rows", [1, NTAB], I32)
        more_pairs = sb("more_pairs", [1, 1], I32)
        gidx = [sb(f"gidx{i}", [P, 1], I32) for i in range(2)]
        sidx = [sb(f"sidx{i}", [P, 1], I32) for i in range(2)]
        with ExitStack() as early:
            def sbe(name, shape):
                return early.enter_context(nc.sbuf_tensor(name, shape, F32))

            ws_g, ws_u, ws_d = sbe("ws_g", [P, DC, FF]), sbe("ws_u", [P, DC, FF]), sbe("ws_d", [P, 2, D])
            w_router, bias = sbe("w_router_sb", [P, DC, E]), sbe("router_bias_sb", [P, E])
            rt = sbe("rt", [P, 8, TJ, E])
            cnt = sbe("cnt", [P, 3, P])
            small = sbe("small", [P, 64])
            chosenT = sbe("chosenT", [P, TJ, P])
            top = sbe("top", [P, TJ * NG, 8])
            sbe("unused", [P, 256])
            act_sT, act_s, sil_s = sbe("act_sT", [P, 2, P]), sbe("act_s", [P, TJ, FF]), sbe("sil_s", [P, FF])
        w_hi = [sb(f"w_hi{n}", [P, 4, 2, FF], F32R) for n in "ab"] + [sb("w_hid", [P, 2, D], F32R)]
        w_lo = [sb(f"w_lo{n}", [P, 4, 2, FF], F32R) for n in "ab"] + [sb("w_lod", [P, 2, D], F32R)]
        hbT_hi, hbT_lo = sb("hbT_hi", [P, DC, P], F32R), sb("hbT_lo", [P, DC, P], F32R)
        actT_hi, actT_lo = sb("actT_hi", [P, 2, P], F32R), sb("actT_lo", [P, 2, P], F32R)
        h2 = [h[:, 0, :], h[:, 1, :]] + [mixT[:, 4 + 2 * i:6 + 2 * i, :].rearrange("p a n -> p (a n)") for i in range(2)]
        hb = [mixT[:, 2 * i:2 * i + 2, :].rearrange("p a n -> p (a n)") for i in range(2)]
        yb = [mixT[:, 4 + 2 * i:6 + 2 * i, :].rearrange("p a n -> p (a n)") for i in range(2)]
        sel = h[:, 0, 512:1024].rearrange("p (j s) -> p j s", j=TJ)
        shared_y = h[:, :, 0:512]
        act_b, sil_b = hT[:, 1, 0:FF], hT[:, 2, 0:FF]

        s_w = sem("s_w")
        d_ws = sem("d_ws")
        s_link, s_h, s_hTps, s_hT = (sem(n) for n in "s_link s_h s_hTps s_hT".split())
        s_h2 = sem("s_h2")
        s_logit, s_score, s_M, s_MT, s_MTe, s_ranks, s_ranked = (sem(n) for n in "s_logit s_score s_M s_MT s_MTe s_ranks s_ranked".split())
        s_count, s_nb, s_cum, s_cume, s_tab, s_table = (sem(n) for n in "s_count s_nb s_cum s_cume s_tab s_table".split())
        s_sgu, s_ssil, s_sact, s_sT, s_sTe, s_sdown, s_sx = (sem(n) for n in "s_sgu s_ssil s_sact s_sT s_sTe s_sdown s_sx".split())
        s_zero, s_started = sem("s_zero"), sem("s_started")
        raw_gu_in, raw_d_in = [sem("raw_gu_in0"), sem("raw_gu_in1")], [sem("raw_d_in0"), sem("raw_d_in1")]
        hi = [sem("hi_a"), sem("hi_b"), sem("hi_d")]
        lo = [sem("lo_a"), sem("lo_b"), sem("lo_d")]
        s_gu_half, s_gu, s_down, s_turn, s_list, s_actT = (sem(n) for n in "s_gu_half s_gu s_down s_turn s_list s_actT".split())
        s_hb_hi, s_hb_lo, s_sil, s_act, s_aT_hi, s_aT_lo = (sem(n) for n in "s_hb_hi s_hb_lo s_sil s_act s_aT_hi s_aT_lo".split())
        s_yout, s_sel, s_gidx, s_sidx, s_gathered, s_scattered = (sem(n) for n in "s_yout s_sel s_gidx s_sidx s_gathered s_scattered".split())
        y_in = [sem("y_in0"), sem("y_in1")]
        s_ysum = sem("s_ysum")

        h2_rows = h2_dram.rearrange("(j p) n -> p j n", p=P)
        y_rows = y_dram.rearrange("(k j p) n -> p k j n", p=P, j=TJ)
        wg, wu, wd = ins["w_gate"], ins["w_up"], ins["w_down"]
        bank_s = [bank[4], bank[6]]
        bank_g, bank_t, bank_y, bank_a, bank_l = bank[0:2], bank[2:4], bank[4:6], bank[6], bank[7]

        def expert_of(eng, s):
            return eng.value_load(block_expert[0:1, bass.ds(s.n, 1)], min_val=0, max_val=E - 1)

        def steps(eng, step):
            for n in range(3):
                step(Step(n // 2, n % 2))
            more = eng.value_load(more_pairs[0:1, 0:1], min_val=MIN_PAIRS - LEAST, max_val=MAX_PAIRS - LEAST) + (LEAST - 1)
            with eng.Fori(1, MAX_PAIRS - 1) as i:
                with eng.If(i < more):
                    step(Step(i, 1))
                    step(Step(i + 1, 0))
            step(Step(more, 1), last=True)
            return Step(more + 1, 0)

        with nc.Block() as block:
            @block.sync
            def _(sp):
                sp.dma_start(w_router[:], dram("w_router", l).rearrange("o (p c) e -> p (o c) e", c=DC)).then_inc(s_w, 16)
                sp.dma_start(bias[:], dram("router_bias", l).to_broadcast([P, E])).then_inc(s_w, 16)
                sp.dma_start(ws_g[:], dram("ws_gate", l).rearrange("o (p c) f -> p (o c) f", c=DC)).then_inc(d_ws, 16)
                sp.dma_start(ws_u[:], dram("ws_up", l).rearrange("o (p c) f -> p (o c) f", c=DC)).then_inc(d_ws, 16)
                sp.dma_start(ws_d[:], dram("ws_down", l).rearrange("o (p c) n -> p (o c) n", c=2)).then_inc(d_ws, 16)
                for j in range(TJ):
                    sp.wait_ge(s_h, j + 1)
                    sp.dma_start(h2_rows[:, j, :], h2[j]).then_inc(s_h2, 16)
                sp.wait_ge(s_table, 1)

                def load_gate_up(s):
                    at = (bass.ds(l, 1), bass.ds(expert_of(sp, s), 1))
                    wait(sp, lo[1], s.n - 1)
                    for k, w in enumerate((wg, wu)):
                        sp.dma_start(raw_gu[s.par][:, k], w[at].rearrange("a b (p c) f -> p (a b c) f", c=DC)).then_inc(raw_gu_in[s.par], 16)

                def load_down(s):
                    at = (bass.ds(l, 1), bass.ds(expert_of(sp, s), 1))
                    wait(sp, lo[2], s.n - 1)
                    sp.dma_start(raw_d[s.par][:], wd[at].rearrange("a b (p c) n -> p (a b c) n", c=2)).then_inc(raw_d_in[s.par], 16)

                def step(s, last=False):
                    if not last:
                        load_gate_up(s + 1)
                    load_down(s)

                load_gate_up(Step(0, 0))
                end = steps(sp, step)
                sp.wait_ge(s_scattered, end.n)
                for j in range(TJ):
                    for half in range(2):
                        u = 2 * j + half
                        wait(sp, s_ysum, u - 1)
                        sp.dma_start(raw_gu[half][:].rearrange("p a c f -> p (a c f)").rearrange("p (k n) -> p k n", k=4),
                                     y_rows[:, 4 * half:4 * half + 4, j, :]).then_inc(y_in[half], 16)

            @block.gpsimd
            def _(pool):
                bound_h, bound_y = pool.to_reg(T - 1), pool.to_reg(TOPK * T - 1)
                for i in range(2):
                    pool.memset(hb[i], 0.0).then_inc(s_zero, 1)
                pool.wait_ge(s_zero, 2)
                pool.wait_ge(s_h2, 16 * TJ)
                before = pool.snap(cum_pairs, min_val=0, max_val=DEPTH * (MAX_PAIRS + 1))

                def by_rows(s, move):
                    rows = pool.value_load(block_rows[0:1, bass.ds(s.n, 1)], min_val=0, max_val=T)
                    with pool.If(rows < P // 2 + 1):
                        with pool.If(rows < P // 4 + 1):
                            move(P // 4)
                        with pool.Else():
                            move(P // 2)
                    with pool.Else():
                        with pool.If(rows < 3 * P // 4 + 1):
                            move(3 * P // 4)
                        with pool.Else():
                            move(P)

                def gather(s):
                    wait(pool, s_turn, s.n - 1)
                    pool.wait_ge(s_gidx, s.n + 1)
                    pool.nop().then_inc(s_started, 1)
                    by_rows(s, lambda rows: pool.indirect_dma_start(
                        out=hb[s.par][0:rows], out_offset=None, in_=h2_dram,
                        in_offset=bass.IndirectOffsetOnAxis(ap=gidx[s.par][0:rows, 0:1].bitcast(U32), axis=0),
                        bounds_check=bound_h, oob_is_err=False).then_inc(gathered_dma[s.par], 16))

                def gathered(s):
                    pool.wait_ge(gathered_dma[s.par], (before + s.half + 1 + (l if s.par == 0 else 0)) * 16)
                    pool.nop().then_inc(s_gathered, 1)

                def scatter(s):
                    pool.wait_ge(s_sidx, s.n + 1)
                    pool.wait_ge(s_yout, s.n + 1)
                    pool.nop().then_inc(s_started, 1)
                    by_rows(s, lambda rows: pool.indirect_dma_start(
                        out=y_dram, in_=yb[s.par][0:rows], in_offset=None,
                        out_offset=bass.IndirectOffsetOnAxis(ap=sidx[s.par][0:rows, 0:1].bitcast(U32), axis=0),
                        bounds_check=bound_y, oob_is_err=False).then_inc(scattered_dma[s.par], 16))

                def scattered(s):
                    pool.wait_ge(scattered_dma[s.par], (before + s.half + 1) * 16)
                    pool.nop().then_inc(s_scattered, 1)

                gather(Step(0, 0))
                gather(Step(0, 1))

                def step(s, last=False):
                    gathered(s + 1)
                    if not last:
                        gather(s + 2)
                    if later(s, 2):
                        scattered(s + -2)
                    if later(s, 1):
                        scatter(s + -1)

                gathered(Step(0, 0))
                end = steps(pool, step)
                scattered(end + -2)
                scatter(end + -1)
                scattered(end + -1)
                pool.reg_add(cum_pairs, cum_pairs, pool.to_reg(end.half))

            @block.scalar
            def _(act):
                for j in range(TJ):
                    act.wait_ge(s_hTps, j + 1)
                    for b in range(2):
                        i = act.activation(hT[:, 4 * b:4 * b + 4, j * P:j * P + P],
                                           bank[2 * (j % 2) + b][:].rearrange("p (c t) -> p c t", c=4), ACT.Copy)
                    i.then_inc(s_hT, 1)
                act.wait_ge(s_logit, 1)
                act.activation(rt[:, 0], bank[4][:, 0:TJ * E].rearrange("p (j e) -> p j e", j=TJ), ACT.Sigmoid).then_inc(s_score, 1)
                for j in range(TJ):
                    act.wait_ge(s_sgu, j + 1)
                    wait(act, s_sact, j)
                    act.activation(sil_s[:], bank[j % 2][:, 0:FF], ACT.Silu).then_inc(s_ssil, 1)

                def shared_turned(j):
                    act.wait_ge(s_sT, j + 1)
                    wait(act, s_sdown, 2 * j)
                    act.activation(act_sT[:], bank[5][:, 0:2 * P].rearrange("p (c t) -> p c t", c=2), ACT.Copy).then_inc(s_sTe, 1)

                def part_hi(k, s):
                    act.wait_ge((raw_gu_in, raw_gu_in, raw_d_in)[k][s.par], (s.half + 1) * (32 if k < 2 else 16))
                    if k < 2:
                        act.activation(w_hi[k][:].rearrange("p c g f -> p g c f"), raw_gu[s.par][:, :, 4 * k:4 * k + 4, :], ACT.Copy).then_inc(hi[k], 1)
                    else:
                        act.activation(w_hi[2][:], raw_d[s.par][:], ACT.Copy).then_inc(hi[2], 1)

                def turned_hi(s):
                    act.wait_ge(s_turn, s.n + 1)
                    wait(act, s_gu, s.n)
                    for b in range(2):
                        i = act.activation(hbT_hi[:, 4 * b:4 * b + 4, :], bank_t[b][:].rearrange("p (c t) -> p c t", c=4), ACT.Copy)
                    i.then_inc(s_hb_hi, 1)

                def y_out(s):
                    act.wait_ge(s_down, s.n + 1)
                    wait(act, s_scattered, s.n - 1)
                    for b in range(2):
                        i = act.activation(yb[s.par][:, 512 * b:512 * b + 512], bank_y[b][:], ACT.Copy)
                    i.then_inc(s_yout, 1)

                shared_turned(0)
                part_hi(0, Step(0, 0))
                shared_turned(1)
                part_hi(1, Step(0, 0))
                turned_hi(Step(0, 0))
                shared_turned(2)
                shared_turned(3)

                def step(s, last=False):
                    act.wait_ge(s_gu_half, s.n + 1)
                    if not last:
                        part_hi(0, s + 1)
                    act.wait_ge(s_gu, s.n + 1)
                    wait(act, s_act, s.n)
                    act.activation(sil_b, bank_g[s.par][:, 0:FF], ACT.Silu).then_inc(s_sil, 1)
                    if not last:
                        part_hi(1, s + 1)
                        turned_hi(s + 1)
                    if later(s, 1):
                        y_out(s + -1)
                    part_hi(2, s)
                    act.wait_ge(s_actT, s.n + 1)
                    act.activation(actT_hi[:], bank_a[:, 0:2 * P].rearrange("p (c t) -> p c t", c=2), ACT.Copy).then_inc(s_aT_hi, 1)

                end = steps(act, step)
                y_out(end + -1)

            @block.vector
            def _(dve):
                links = [0]

                def link(i):
                    links[0] += 1
                    i.then_inc(s_link, 1)
                    dve.wait_ge(s_link, links[0])

                link(dve.reciprocal(stat[:, 8:12], stat[:, 20:24]))
                for j in range(TJ):
                    link(dve.scalar_tensor_tensor(out=h2[j], in0=x[:, j, :], scalar=stat[:, 8 + j:9 + j], in1=mod[:, SCALE2, :], op0=ALU.mult, op1=ALU.mult))
                    dve.tensor_tensor(h2[j], h2[j], mod[:, SHIFT2, :], ALU.add).then_inc(s_h, 1)

                def shared_act(j):
                    dve.wait_ge(s_ssil, j + 1)
                    dve.tensor_tensor(act_s[:, j, :], bank[j % 2][:, FF:2 * FF], sil_s[:], ALU.mult).then_inc(s_sact, 1)

                def shared_sum(j):
                    for b in range(2):
                        dve.wait_ge(s_sdown, 2 * j + b + 1)
                        link(dve.tensor_tensor(shared_y[:, b, :], bank_s[b][:], mod[:, GATE2, 512 * b:512 * b + 512], ALU.mult))
                        dve.tensor_tensor(x[:, j, 512 * b:512 * b + 512], x[:, j, 512 * b:512 * b + 512], shared_y[:, b, :], ALU.add).then_inc(s_sx, 1)

                score, sel_score, junk, chosen, weight, left = (rt[:, k] for k in range(6))
                grouped = [P, TJ, NG, PER_G]

                def by_group(a):
                    return a.rearrange("p j (g e) -> p j g e", g=NG)

                dve.wait_ge(s_score, 1)
                dve.wait_ge(s_w, 32)
                link(dve.tensor_tensor(sel_score, score, bias[:].unsqueeze(1).to_broadcast([P, TJ, E]), ALU.add))
                for j in range(TJ):
                    for g in range(NG):
                        i = dve.max(top[:, j * NG + g, :], sel_score[:, j, g * PER_G:g * PER_G + PER_G])
                link(i)
                group = small[:, 0:TJ * NG].rearrange("p (j g) -> p j g", j=TJ)
                link(dve.tensor_tensor(small[:, 0:TJ * NG], top[:, :, 0], top[:, :, 1], ALU.add))
                better, ties = junk, left
                this = group.unsqueeze(3).to_broadcast(grouped)
                for j in range(TJ):
                    this, other = group[:, j, :].unsqueeze(2).to_broadcast([P, NG, NG]), group[:, j, :].unsqueeze(1).to_broadcast([P, NG, NG])
                    dve.tensor_tensor(by_group(better)[:, j], other, this, ALU.is_gt)
                    i = dve.tensor_tensor(by_group(ties)[:, j], other, this, ALU.is_equal)
                link(i)
                link(dve.tensor_tensor(ties, ties, cst("lower_group").unsqueeze(1).to_broadcast([P, TJ, E]), ALU.mult))
                link(dve.tensor_tensor(better, better, ties, ALU.add))
                keep = small[:, 32:64].rearrange("p (j g) -> p j g", j=TJ)
                link(dve.tensor_reduce(small[:, 32:64], better.rearrange("p j (g e) -> p (j g) e", g=NG), AX, ALU.add))
                link(dve.tensor_scalar(small[:, 32:64], small[:, 32:64], float(TOPG), None, ALU.is_lt))
                link(dve.tensor_scalar(small[:, 0:32], small[:, 32:64], -MASKED, MASKED, ALU.mult, ALU.add))

                def spread(a):
                    return a.rearrange("p (q o) -> p q o", o=1).to_broadcast([P, TJ * NG, PER_G])

                flat = [a.rearrange("p j (g e) -> p (j g) e", g=NG) for a in (sel_score, left)]
                link(dve.tensor_tensor(flat[0], flat[0], spread(small[:, 32:64]), ALU.mult))
                link(dve.tensor_tensor(flat[0], flat[0], spread(small[:, 0:32]), ALU.add))
                for j in range(TJ):
                    link(dve.max(top[:, j, :], sel_score[:, j, :]))
                    i = dve.match_replace(out=left[:, j, :], in_to_replace=top[:, j, :], in_values=sel_score[:, j, :], imm_value=TAKEN)
                link(i)
                dve.tensor_scalar(chosen, left, (TAKEN + MASKED) / 2, None, ALU.is_lt).then_inc(s_M, 1)
                dve.wait_ge(s_M, 1)
                link(dve.tensor_tensor(weight, score, chosen, ALU.mult))
                link(dve.tensor_reduce(small[:, 0:TJ], weight, AX, ALU.add))
                link(dve.reciprocal(small[:, 4:8], small[:, 0:TJ]))
                link(dve.tensor_scalar(small[:, 4:8], small[:, 4:8], 2.5, None, ALU.mult))
                dve.tensor_tensor(meta[:, :, :, 2], weight, small[:, 4:8].unsqueeze(2).to_broadcast([P, TJ, E]), ALU.mult)
                shared_act(0)
                shared_act(1)
                dve.wait_ge(s_count, 1)
                link(dve.tensor_scalar(small[0:E, 8:12], cst("steps", E), bank[5][0:E, 256:257], None, ALU.is_lt))
                link(dve.tensor_copy(small[0:E, 14:15], bank[5][0:E, 256:257]))
                link(dve.tensor_reduce(small[0:E, 12:13], small[0:E, 8:12], AX, ALU.add))
                dve.tensor_scalar(cnt[0:E, 0, :], ones[0:E, :], small[0:E, 12:13], None, ALU.mult).then_inc(s_nb, 1)
                dve.wait_ge(s_MT, 1)
                dve.tensor_copy(chosenT[0:E], bank[7][0:E, :].rearrange("p (j t) -> p j t", j=TJ)).then_inc(s_MTe, 1)
                dve.wait_ge(s_cum, 1)
                link(dve.tensor_copy(small[0:E, 13:14], bank[5][0:E, 257:258]))
                link(dve.tensor_tensor(small[0:E, 15:16], small[0:E, 13:14], small[0:E, 12:13], ALU.subtract))
                link(dve.tensor_scalar(cnt[0:E, 2, 0:NTAB], cst("block", E), small[0:E, 15:16], None, ALU.is_ge))
                link(dve.tensor_scalar(cnt[0:E, 1, 0:NTAB], cst("block", E), small[0:E, 13:14], None, ALU.is_ge))
                dve.tensor_tensor(cnt[0:E, 2, 0:NTAB], cnt[0:E, 2, 0:NTAB], cnt[0:E, 1, 0:NTAB], ALU.subtract).then_inc(s_cume, 1)
                dve.wait_ge(s_ranks, 1)
                for j in range(TJ):
                    link(dve.tensor_tensor(junk[:, j, :], bank[6][:, j * E:j * E + E], chosen[:, j, :], ALU.mult))
                link(dve.tensor_scalar(left, chosen, -NO_SLOT, NO_SLOT, ALU.mult, ALU.add))
                link(dve.tensor_tensor(rank[:].rearrange("p e j -> p j e"), junk, left, ALU.add))
                dve.wait_ge(s_tab, 1)
                link(dve.tensor_scalar(cnt[:, 2, 0:NTAB], bank[7][:, 0:NTAB], float(E), None, ALU.is_equal))
                link(dve.tensor_scalar(small[:, 16:17], bank[7][:, 2 * P:2 * P + 1], 0.0, None, ALU.add))
                link(dve.tensor_scalar(rt[:, 7].rearrange("p j e -> p (j e)")[:, 0:NTAB], bank[7][:, 0:NTAB], float(E - 1), None, ALU.min))
                link(dve.tensor_copy(block_expert[:], rt[0:1, 7].rearrange("p j e -> p (j e)")[:, 0:NTAB]))
                link(dve.tensor_tensor(rank_off[:], cst("block"), bank[7][:, P:P + NTAB], ALU.subtract))
                link(dve.scalar_tensor_tensor(out=rank_off[:], in0=cnt[:, 2, 0:NTAB], scalar=64.0, in1=rank_off[:], op0=ALU.mult, op1=ALU.add))
                link(dve.tensor_scalar(rank_off[:], rank_off[:], float(P), None, ALU.mult))
                link(dve.tensor_tensor(cnt[0:1, 2, 0:NTAB], bank[7][0:1, 3 * P:3 * P + NTAB], rank_off[0:1, :], ALU.subtract))
                link(dve.tensor_scalar(block_rows[:], cnt[0:1, 2, 0:NTAB], 0.0, None, ALU.max))
                link(dve.tensor_scalar(cnt[:, 2, 0:MAX_PAIRS + 1], cst("even"), small[:, 16:17], None, ALU.is_lt))
                link(dve.tensor_reduce(small[:, 17:18], cnt[:, 2, 0:MAX_PAIRS + 1], AX, ALU.add))
                link(dve.tensor_scalar(more_pairs[:], small[0:1, 17:18], -float(LEAST), None, ALU.add))
                dve.wait_ge(s_ranks, 2)
                for j in range(TJ):
                    dve.tensor_scalar(meta[:, j, :, 1], bank[4][:, j * E:j * E + E], float(T), cst("token")[:, j:j + 1], ALU.mult, ALU.add)
                    i = dve.tensor_scalar(meta[:, j, :, 0], chosen[:, j, :], 0.0, cst("token")[:, j:j + 1], ALU.mult, ALU.add)
                i.then_inc(s_table, 1)
                def select(s):
                    e = expert_of(dve, s)
                    wait(dve, s_list, s.n)
                    dve.scalar_tensor_tensor(out=sel, in0=cst("slots").unsqueeze(1).to_broadcast([P, TJ, P]),
                                             scalar=rank_off[:, bass.ds(s.n, 1)],
                                             in1=rank[:, bass.ds(e, 1), :].rearrange("p e j -> p (e j)").unsqueeze(2).to_broadcast([P, TJ, P]),
                                             op0=ALU.add, op1=ALU.is_equal).then_inc(s_sel, 1)

                def listing(s):
                    dve.wait_ge(s_list, s.n + 1)
                    wait(dve, s_gathered, s.n - 1)
                    dve.tensor_copy(listed[:, bass.ds(s.n, 1), :].rearrange("p b k -> p (b k)"), bank_l[:, 0:3])
                    dve.tensor_scalar(gidx[s.par][:], bank_l[:, 0:1], NO_SLOT, None, ALU.add).then_inc(s_gidx, 1)

                def part_lo(k, s):
                    dve.wait_ge(hi[k], s.n + 1)
                    if k < 2:
                        dve.tensor_tensor(w_lo[k][:].rearrange("p c g f -> p g c f"), raw_gu[s.par][:, :, 4 * k:4 * k + 4, :],
                                          w_hi[k][:].bitcast(F32).rearrange("p c g f -> p g c f"), ALU.subtract).then_inc(lo[k], 1)
                    else:
                        dve.tensor_tensor(w_lo[2][:], raw_d[s.par][:], w_hi[2][:].bitcast(F32), ALU.subtract).then_inc(lo[2], 1)

                def turned_lo(s):
                    dve.wait_ge(s_hb_hi, s.n + 1)
                    for b in range(2):
                        i = dve.tensor_tensor(hbT_lo[:, 4 * b:4 * b + 4, :], bank_t[b][:].rearrange("p (c t) -> p c t", c=4),
                                              hbT_hi[:, 4 * b:4 * b + 4, :].bitcast(F32), ALU.subtract)
                    i.then_inc(s_hb_lo, 1)

                dve.wait_ge(s_h2, 16 * TJ)
                for n in range(2):
                    select(Step(0, n))
                    shared_act(2 + n)
                    listing(Step(0, n))
                select(Step(1, 0))
                shared_sum(0)
                part_lo(0, Step(0, 0))
                shared_sum(1)
                part_lo(1, Step(0, 0))
                turned_lo(Step(0, 0))
                shared_sum(2)
                shared_sum(3)

                def step(s, last=False):
                    if not last:
                        part_lo(0, s + 1)
                        listing(s + 2)
                    dve.wait_ge(s_sil, s.n + 1)
                    wait(dve, s_actT, s.n)
                    dve.wait_ge(s_gidx, s.n + 1)
                    dve.scalar_tensor_tensor(out=act_b, in0=bank_g[s.par][:, FF:2 * FF], scalar=listed[:, bass.ds(s.n, 1), 2],
                                             in1=sil_b, op0=ALU.mult, op1=ALU.mult).then_inc(s_act, 1)
                    if not last:
                        turned_lo(s + 1)
                        part_lo(1, s + 1)
                        select(s + 3)
                    part_lo(2, s)
                    dve.wait_ge(s_aT_hi, s.n + 1)
                    dve.tensor_tensor(actT_lo[:], bank_a[:, 0:2 * P].rearrange("p (c t) -> p c t", c=2), actT_hi[:].bitcast(F32), ALU.subtract).then_inc(s_aT_lo, 1)
                    wait(dve, s_scattered, s.n - 1)
                    dve.tensor_scalar(sidx[s.par][:], listed[:, bass.ds(s.n, 1), 1], NO_SLOT, None, ALU.add).then_inc(s_sidx, 1)

                steps(dve, step)
                for j in range(TJ):
                    r = [raw_gu[k][:].rearrange("p a c f -> p (a c f)").rearrange("p (k n) -> p k n", k=4) for k in range(2)]
                    for half in range(2):
                        dve.wait_ge(y_in[half], 16 * (j + 1))
                        link(dve.tensor_tensor(r[half][:, 0:2], r[half][:, 0:2], r[half][:, 2:4], ALU.add))
                        to = yb[half]
                        dve.tensor_tensor(to, r[half][:, 0], r[half][:, 1], ALU.add).then_inc(s_ysum, 1)
                    dve.wait_ge(s_ysum, 2 * j + 2)
                    link(dve.tensor_tensor(yb[0], yb[0], yb[1], ALU.add))
                    link(dve.tensor_tensor(yb[0], yb[0], mod[:, GATE2, :], ALU.mult))
                    link(dve.tensor_tensor(x[:, j, :], x[:, j, :], yb[0], ALU.add))

            @block.tensor
            def _(pe):
                def turn_tokens(j):
                    pe.wait_ge(s_h, j + 1)
                    wait(pe, s_hT, j - 1)
                    for c in range(DC):
                        i = pe.transpose(bank[2 * (j % 2) + c // 4][:, (c % 4) * P:(c % 4) * P + P], h2[j][:, c:D:DC], ident)
                    i.then_inc(s_hTps, 1)

                def logits(j):
                    pe.wait_ge(s_hT, j + 1)
                    for c in range(DC):
                        i = pe.matmul(bank[4][:, j * E:j * E + E], hT[:, c, j * P:j * P + P], w_router[:, c, :], start=c == 0, stop=c == DC - 1)
                    return i

                turn_tokens(0)
                pe.wait_ge(s_w, 32)
                for j in range(1, TJ):
                    turn_tokens(j)
                    logits(j - 1)
                logits(TJ - 1).then_inc(s_logit, 1)

                def shared(j):
                    wait(pe, s_sact, j - 1)
                    for k, w in enumerate((ws_g, ws_u)):
                        for c in range(DC):
                            i = pe.matmul(bank[j % 2][:, k * FF:k * FF + FF], hT[:, c, j * P:j * P + P], w[:, c, :], start=c == 0, stop=c == DC - 1)
                    i.then_inc(s_sgu, 1)

                def shared_down(j):
                    pe.wait_ge(s_sact, j + 1)
                    wait(pe, s_sTe, j)
                    for c in range(2):
                        i = pe.transpose(bank[5][:, c * P:c * P + P], act_s[:, j, c:FF:2], ident)
                    i.then_inc(s_sT, 1)
                    pe.wait_ge(s_sTe, j + 1)
                    for b in range(2):
                        wait(pe, s_sx, 2 * (j - 1) + b + 1)
                        for c in range(2):
                            i = pe.matmul(bank_s[b][:], act_sT[:, c, :], ws_d[:, c, 512 * b:512 * b + 512], start=c == 0, stop=c == 1)
                        i.then_inc(s_sdown, 1)

                pe.wait_ge(d_ws, 48)
                shared(0)
                shared(1)
                chosen = rt[:, 3]
                pe.wait_ge(s_M, 1)
                for j in range(TJ):
                    i = pe.matmul(bank[5][0:E, 256:257], chosen[:, j, :], ones[:, 0:1], start=j == 0, stop=j == TJ - 1)
                i.then_inc(s_count, 1)
                for j in range(TJ):
                    for k in range(j + 1):
                        i = pe.matmul(bank[6][:, j * E:j * E + E], cst("before") if k == j else ones, chosen[:, k, :], start=k == 0, stop=k == j)
                i.then_inc(s_ranks, 1)
                for j in range(TJ):
                    i = pe.transpose(bank[7][0:E, j * P:j * P + P], chosen[:, j, :], ident)
                i.then_inc(s_MT, 1)
                pe.wait_ge(s_nb, 1)
                pe.matmul(bank[5][0:E, 257:258], cst("upto", E)[:, 0:E], cnt[0:E, 0, 0:1], start=True, stop=True).then_inc(s_cum, 1)
                shared(2)
                pe.wait_ge(s_MTe, 1)
                pe.wait_ge(s_score, 1)
                for j in range(TJ):
                    i = pe.matmul(bank[4][:, j * E:j * E + E], chosenT[0:E, j, :], cst("before", E)[:, 0:E], start=True, stop=True)
                i.then_inc(s_ranks, 1)
                pe.wait_ge(s_cume, 1)
                pe.matmul(bank[7][:, 0:NTAB], ones[0:E, :], cnt[0:E, 1, 0:NTAB], start=True, stop=True)
                pe.matmul(bank[7][:, P:P + NTAB], cnt[0:E, 0, :], cnt[0:E, 1, 0:NTAB], start=True, stop=True)
                pe.matmul(bank[7][0:1, 3 * P:3 * P + NTAB], small[0:E, 14:15], cnt[0:E, 2, 0:NTAB], start=True, stop=True)
                pe.matmul(bank[7][:, 2 * P:2 * P + 1], cnt[0:E, 0, :], ones[0:E, 0:1], start=True, stop=True).then_inc(s_tab, 1)
                shared(3)

                def list_block(s):
                    e = expert_of(pe, s)
                    pe.wait_ge(s_sel, s.n + 1)
                    wait(pe, s_gidx, s.n)
                    for j in range(TJ):
                        i = pe.matmul(bank_l[:, 0:3], sel[:, j, :], meta[:, j, bass.ds(e, 1), :].rearrange("p e k -> p (e k)"), start=j == 0, stop=j == TJ - 1)
                    i.then_inc(s_list, 1)

                def turn(s):
                    pe.wait_ge(s_gathered, s.n + 1)
                    wait(pe, s_hb_lo, s.n)
                    for c in range(DC):
                        i = pe.transpose(bank_t[c // 4][:, (c % 4) * P:(c % 4) * P + P], hb[s.par][:, c:D:DC], ident)
                    i.then_inc(s_turn, 1)

                def product(dst, a_hi, a_lo, b_hi, b_lo, first, last):
                    pe.matmul(dst, a_hi, b_hi, start=first, stop=False)
                    pe.matmul(dst, a_hi, b_lo, start=False, stop=False)
                    return pe.matmul(dst, a_lo, b_hi, start=False, stop=last)

                def gate_up(s):
                    pe.wait_ge(s_hb_lo, s.n + 1)
                    wait(pe, s_act, s.n - 1)
                    for k in range(2):
                        pe.wait_ge(lo[k], s.n + 1)
                        for c in range(4):
                            cc = 4 * k + c
                            i = product(bank_g[s.par][:], hbT_hi[:, cc, :], hbT_lo[:, cc, :],
                                        w_hi[k][:, c].rearrange("p g f -> p (g f)"), w_lo[k][:, c].rearrange("p g f -> p (g f)"), cc == 0, cc == DC - 1)
                        i.then_inc((s_gu_half, s_gu)[k], 1)

                def down(s):
                    pe.wait_ge(s_aT_lo, s.n + 1)
                    pe.wait_ge(lo[2], s.n + 1)
                    wait(pe, s_yout, s.n)
                    for c in range(2):
                        for b in range(2):
                            w = slice(512 * b, 512 * b + 512)
                            i = product(bank_y[b][:], actT_hi[:, c, :], actT_lo[:, c, :], w_hi[2][:, c, w], w_lo[2][:, c, w], c == 0, c == 1)
                    i.then_inc(s_down, 1)

                def turn_act(s):
                    pe.wait_ge(s_act, s.n + 1)
                    wait(pe, s_aT_lo, s.n)
                    if not later(s, 1):
                        pe.wait_ge(s_sx, 2 * TJ)
                    for c in range(2):
                        i = pe.transpose(bank_a[:, c * P:c * P + P], act_b[:, c:FF:2], ident)
                    i.then_inc(s_actT, 1)

                pe.wait_ge(s_table, 1)
                list_block(Step(0, 0))
                list_block(Step(0, 1))
                shared_down(0)
                shared_down(1)
                turn(Step(0, 0))
                shared_down(2)
                shared_down(3)

                def step(s, last=False):
                    gate_up(s)
                    if not last:
                        list_block(s + 2)
                        turn(s + 1)
                    if later(s, 1):
                        down(s + -1)
                    turn_act(s)

                end = steps(pe, step)
                down(end + -1)
        clear(nc, sems)


_NAMES = ["x", "c", "positions", "w_ada", "b_ada", "w_in", "w_pool", "pool_scale", "w_spatial", "b_spatial", "g_q", "w_uq",
          "g_kv", "w_ukv", "w_out", "w_router", "router_bias", "w_gate", "w_up", "w_down", "ws_gate", "ws_up", "ws_down",
          "final_gain"]


def kernel(**inputs):
    import concourse.bacc as bacc
    from concourse.bass_utils import run_bass_kernel_spmd

    arrays = {n: np.ascontiguousarray(inputs[n]) for n in _NAMES}
    arrays["const"] = lay_constants()
    nc = bacc.Bacc("TRN2", target_bir_lowering=False, num_devices=1)
    ins = {n: nc.dram_tensor(f"in_{n}", a.shape, mybir.dt.from_np(a.dtype), kind="ExternalInput").ap() for n, a in arrays.items()}
    out = nc.dram_tensor("out_0", (1, T, D), F32, kind="ExternalOutput").ap()
    h2_rows = nc.dram_tensor("h2_rows", (T, D), F32, kind="Internal").ap()
    y_rows = nc.dram_tensor("y_rows", (TOPK * T, D), F32, kind="Internal").ap()
    trunk(nc, ins, out, (h2_rows, y_rows))
    r = run_bass_kernel_spmd(nc, [{f"in_{n}": a for n, a in arrays.items()}], core_ids=[0])
    return r.results[0]["out_0"]
```

```python
from contextlib import ExitStack

import numpy as np

import concourse.bass as bass
from concourse import mybir

ALU = mybir.AluOpType
ACT = mybir.ActivationFunctionType
AX = mybir.AxisListType.X
F32 = mybir.dt.float32
F32R = mybir.dt.float32r
BF16 = mybir.dt.bfloat16
I32 = mybir.dt.int32
U32 = mybir.dt.uint32

P = 128
D = 1024
DC = D // P
T = 512
TJ = T // P
DEPTH = 2
WINDOWS = (2, 4, 8, 16)
GROUP = 64
HEADS, NOPE, ROPE, VDIM = 8, 64, 32, 64
QK = NOPE + ROPE
SCALE = QK ** -0.5
SGH = 4
NIN = 1184
COL_A, COL_U, COL_V, COL_CQ, COL_CKV, COL_PE = 0, 256, 512, 768, 1024, 1152
QL = 256
E, TOPK, NG, PER_G, TOPG = 64, 8, 8, 8, 4
FF = 256
EPS = 1e-6
MAX_BLOCKS = T * TOPK // P + E * (P - 1) // P
MAX_PAIRS = (MAX_BLOCKS + 1) // 2
MIN_PAIRS = T * TOPK // P // 2
MOVED = (16, 32, 48, 64, 80, 96, 112, P)
RUN = 4
RUNS = -(-(MAX_PAIRS - 2) // RUN)
LEAST = 4
NTAB = 2 * RUNS * RUN + 6
NO_SLOT = 65536.0
MASKED = -1.0e30
TAKEN = -2.0e30
PI = float(np.pi)

CONST = {}


def lay_constants():
    parts, at = [], 0

    def put(name, a):
        nonlocal at
        a = np.asarray(a, np.float32).reshape(a.shape[0], -1)
        full = np.zeros((P, a.shape[1]), np.float32)
        full[: a.shape[0]] = a
        CONST[name] = (at, a.shape[1])
        parts.append(full)
        at += a.shape[1]

    k, t = np.arange(P)[:, None], np.arange(P)[None, :]
    put("ident", np.eye(P))
    put("ones", np.ones((P, P)))
    put("before", k < t)
    put("upto", k <= t)
    put("causal", np.where(t <= k, 0.0, MASKED))
    band = np.zeros((P, 4, 3, P))
    for g, w in enumerate(WINDOWS):
        inside = (k <= t) & (k > t - w)
        band[:, g, 0] = inside / np.minimum(t + 1, w) - (k == t)
        band[:, g, 1] = inside / w - (k == t)
        band[:, g, 2] = (k - P > t - w) / w
    put("band", band)
    put("slots", np.broadcast_to(t, (P, P)))
    put("lower_group", np.broadcast_to(np.arange(8)[None, :] < np.arange(8)[:, None], (P, 8, 8)))
    put("token", k + P * np.arange(TJ)[None, :] - NO_SLOT)
    put("block", np.broadcast_to(np.arange(NTAB), (P, NTAB)))
    put("even", np.broadcast_to(2 * np.arange(MAX_PAIRS + 1), (P, MAX_PAIRS + 1)))
    put("steps", np.broadcast_to(P * np.arange(TJ), (P, TJ)))
    freq = (10000.0 ** (-np.arange(0, ROPE, 2, dtype=np.float64) / ROPE)).astype(np.float32)
    put("freq", np.concatenate([np.zeros(NOPE), freq, freq, freq, freq])[:, None])
    put("eps", np.full((P, 1), EPS))
    put("zero", np.zeros((P, 1)))
    return np.concatenate(parts, axis=1)


lay_constants()
NCONST = sum(n for _, n in CONST.values())


def wait(eng, sem, value):
    if isinstance(value, int) and value <= 0:
        return
    eng.wait_ge(sem, value)


def later(s, n):
    return not isinstance(s.n, int) or s.n >= n


class Step:

    def __init__(self, half, par):
        self.half, self.par = half, par
        self.n = half * 2 + par

    def __add__(self, k):
        return Step(self.half + (self.par + k) // 2, (self.par + k) % 2)


def trunk(nc, ins, out, scratch):
    x_in, c_in, positions = ins["x"], ins["c"], ins["positions"]
    h2_dram, y_dram = scratch
    stack = ExitStack()
    with stack:
        def sb_in(where, name, shape, dt=F32):
            return where.enter_context(nc.sbuf_tensor(name, shape, dt))

        def sb(name, shape, dt=F32):
            return sb_in(stack, name, shape, dt)

        def sem(name):
            return stack.enter_context(nc.semaphore(name))

        def sb_both(where, name, shape):
            with nc.sbuf_tensor(name, shape, F32) as plain:
                pass
            return plain, sb_in(where, name + "_r", shape, F32R)

        const = sb("const", [P, NCONST])

        def cst(name, rows=P):
            at, n = CONST[name]
            return const[0:rows, at:at + n]

        ident, ones = cst("ident"), cst("ones")
        x = sb("x", [P, TJ, D])
        mod, mod_r = sb_both(stack, "mod", [P, 6, D])
        rotary = sb("rotary", [P, 2, T])
        cos, sin = rotary[:, 0, :], rotary[:, 1, :]
        h = sb("h", [P, 2, D])
        hT, hT_r = sb_both(stack, "hT", [P, DC, T])
        mixT, mixT_r = sb_both(stack, "mixT", [P, DC, T])
        stat = sb("stat", [P, 32])
        identb = sb("identb", [P, P], BF16)
        causalb = sb("causalb", [P, P], BF16)
        SHIFT1, SCALE1, GATE1, SHIFT2, SCALE2, GATE2 = range(6)
        bank = [stack.enter_context(nc.psum_tensor(f"bank{i}", [P, 512], F32)) for i in range(8)]

        def dram(name, l):
            return ins[name][bass.ds(l, 1)]

        gathered_dma = [sem(f"gathered_dma{i}") for i in range(2)]
        scattered_dma = [sem(f"scattered_dma{i}") for i in range(2)]
        s_start, s_x_in, s_x_square = sem("s_start"), sem("s_x_in"), sem("s_x_square")
        s_final_load, s_final, s_out = sem("s_final_load"), sem("s_final"), sem("s_out")

        start_block = nc.Block()
        with start_block as block:
            @block.sync
            def _(sp):
                sp.dma_start(hT[:, 0, :].bitcast(I32), positions.to_broadcast([P, T])).then_inc(s_start, 16)
                sp.dma_start(const[:], ins["const"]).then_inc(s_start, 16)
                sp.dma_start(x[:], x_in.rearrange("o (j p) n -> p (o j) n", p=P)).then_inc(s_x_in, 16)

            @block.vector
            def _(dve):
                done = [32]

                def link(i):
                    done[0] += 1
                    i.then_inc(s_start, 1)
                    dve.wait_ge(s_start, done[0])

                dve.wait_ge(s_start, 32)
                link(dve.tensor_copy(identb[:], ident))
                link(dve.tensor_copy(causalb[:], cst("causal")))
                ang, turns, red = hT[:, 1, :], hT[:, 2, :], hT[:, 3, :]
                link(dve.tensor_copy(red, hT[:, 0, :].bitcast(I32)))
                link(dve.tensor_scalar(ang, red, cst("freq"), None, ALU.mult))
                MAGIC = 1.5 * 2.0 ** 23
                TURN1, TURN2 = 6.28125, float(np.float32(2 * np.pi - 6.28125))
                for shift, to in ((0.0, sin), (0.25, cos)):
                    link(dve.tensor_scalar(turns, ang, 1.0 / (2 * PI), shift, ALU.mult, ALU.add))
                    link(dve.tensor_scalar(turns, turns, MAGIC, None, ALU.add))
                    link(dve.tensor_scalar(turns, turns, -MAGIC, None, ALU.add))
                    link(dve.scalar_tensor_tensor(out=red, in0=turns, scalar=-TURN1, in1=ang, op0=ALU.mult, op1=ALU.add))
                    link(dve.scalar_tensor_tensor(out=red, in0=turns, scalar=-TURN2, in1=red, op0=ALU.mult, op1=ALU.add))
                    link(dve.tensor_scalar(red, red, shift * 2 * PI, None, ALU.add))
                    link(dve.tensor_scalar(to, red, PI, -PI, ALU.min, ALU.max))

            @block.scalar
            def _(act):
                act.wait_ge(s_x_in, 16)
                act.wait_ge(s_start, 32)
                for j in range(TJ):
                    act.activation(mixT[:, 2 * j:2 * j + 2, :].rearrange("p a n -> p (a n)"), x[:, j, :], ACT.Square,
                                   accum_out=stat[:, 16 + j:17 + j]).then_inc(s_x_square, 1)
                act.wait_ge(s_x_square, TJ)
                act.activation(stat[:, 20:24], stat[:, 16:20], ACT.Sqrt, bias=cst("eps"), scale=1.0 / D).then_inc(s_x_square, 1)
                act.wait_ge(s_start, 32 + 4 + 14)
                act.activation(sin, sin, ACT.Sin).then_inc(s_start, 1)
                act.activation(cos, cos, ACT.Sin).then_inc(s_start, 1)
                act.wait_ge(s_start, 32 + 4 + 16)

        cum_pairs = nc.gpsimd.alloc_register("cum_pairs")
        nc.gpsimd.reg_mov(cum_pairs, 0)

        layers = stack.enter_context(ExitStack())
        l = layers.enter_context(nc.Fori(0, DEPTH))
        mixer(nc, ins, l, locals())
        experts(nc, ins, l, locals())
        layers.close()

        with nc.Block() as block:
            gain = mod[:, 0, :]

            @block.sync
            def _(sp):
                sp.dma_start(gain, ins["final_gain"].rearrange("(o n) -> o n", o=1).to_broadcast([P, D])).then_inc(s_final_load, 16)
                for j in range(TJ):
                    sp.wait_ge(s_final, 2 + j)
                    sp.dma_start(out.rearrange("o (j p) n -> p (o j) n", p=P)[:, j, :], x[:, j, :]).then_inc(s_out, 16)
                sp.wait_ge(s_out, 16 * TJ)

            @block.vector
            def _(dve):
                dve.reciprocal(stat[:, 8:12], stat[:, 20:24]).then_inc(s_final, 1)
                dve.wait_ge(s_final, 1)
                dve.wait_ge(s_final_load, 16)
                for j in range(TJ):
                    dve.scalar_tensor_tensor(out=x[:, j, :], in0=x[:, j, :], scalar=stat[:, 8 + j:9 + j], in1=gain,
                                             op0=ALU.mult, op1=ALU.mult).then_inc(s_final, 1)


def clear(nc, sems):
    nums = [s.num for s in sems]
    assert max(nums) - min(nums) + 1 == len(nums)
    nc.all_engine_barrier(sems_to_clear=range(min(nums), max(nums) + 1))


def mixer(nc, ins, l, v):
    const, cst, x, mod, cos, sin, h, hT, mixT, stat, bank, dram = (
        v[k] for k in "const cst x mod cos sin h hT mixT stat bank dram".split())
    ident, ones, identb, causalb = v["ident"], v["ones"], v["identb"], v["causalb"]
    mod_r, hT_r, mixT_r, sb_both = v["mod_r"], v["hT_r"], v["mixT_r"], v["sb_both"]
    SHIFT1, SCALE1, GATE1 = 0, 1, 2
    with ExitStack() as stack:
        def sb(name, shape, dt=F32):
            return stack.enter_context(nc.sbuf_tensor(name, shape, dt))

        sems = []

        def sem(name):
            sems.append(stack.enter_context(nc.semaphore(name)))
            return sems[-1]

        w_in, w_in_r = sb_both(stack, "w_in_sb", [P, DC, NIN + ROPE])
        w_out, w_out_lo = (t[:].rearrange("p a b -> p (a b)")[:, 0:DC * D].rearrange("p (m n) -> p m n", m=DC) for t in (w_in, w_in_r))
        w_uq, w_uq_r = sb_both(stack, "w_uq_sb", [P, 2, HEADS, QK + ROPE])
        w_ukv = sb("w_ukv_sb", [P, HEADS, NOPE + VDIM])
        w_sp = sb("w_sp", [P, SGH, P])
        w_spT = sb("w_spT", [P, SGH, P])
        b_sp = sb("b_sp", [1, SGH, P])
        w_pool = sb("w_pool_sb", [P, 2, P])
        pool_scale = sb("pool_scale_sb", [P, 2])
        g_q, g_kv = sb("g_q_sb", [P, 2]), sb("g_kv_sb", [P, 1])
        cond = sb("cond", [P, 2, DC])
        (a_sb, a_r), (v_sb, v_r) = sb_both(stack, "a_sb", [P, TJ, 256]), sb_both(stack, "v_sb", [P, TJ, 256])
        latent = sb("latent", [P, 3, T])
        qk, qk_r = sb_both(stack, "qk", [P, 4, T])
        q_sb, k_sb = qk[0:QK, 0:2, :], qk[0:QK, 2:4, :]
        k_pe = mixT[:, 0:2, :]
        tmp = sb("tmp", [P, 2, T])
        b_row = v["rotary"][0:1, :, :]
        acc = sb("acc", [P, 2, 512])
        w_ada, w_ada_r = sb_both(stack, "w_ada_sb", [P, 2, DC // 2, 512])
        rs = sb("rs", [P, 4 * HEADS * TJ])
        bn = sb("bn", [P, TJ, 8])
        AHEAD = 6
        ada_at = [w_ada[:, 0], w_ada[:, 1], hT[:, 0:4, :], hT[:, 4:8, :], mixT[:, 0:4, :], mixT[:, 4:8, :]]

        def ada_unit(u):
            n = u if u < AHEAD else u % 2
            return ada_at[n], n, 16 if u < AHEAD else 16 * ((u - AHEAD) // 2 + 2)

        v_att = hT[:, 0:4, :].rearrange("p j (h d) -> p j h d", h=HEADS)
        o_att = hT[:, 4:8, :]
        probs = h[:, :, 0:512]
        probsT = h[:, :, 512:1024]
        dT = tmp
        w_out_hi = [[(a_r, v_r)[m // 2][:].rearrange("p j n -> p (j n)").rearrange("p (m n) -> p m n", m=2)[:, m % 2, :] if m < 4
                     else mod_r[:, 0:2, :].rearrange("p k n -> p (k n)")[:, (m - 4) * 512:(m - 3) * 512] for m in range(DC)],
                    [w_ada_r[:, m // 4, m % 4, :] for m in range(DC)]]
        mix_hi = [w_uq_r[:].rearrange("p m h q -> p (m h q)").rearrange("p (m t) -> p m t", m=4), hT_r[:, 0:4, :]]
        mix_lo = mixT_r
        NCOL = NIN + ROPE
        w_in_hi = [mod_r[:].rearrange("p k n -> p (k n)")[:, c * NCOL:(c + 1) * NCOL] if c < 5
                   else w_ada_r[:].rearrange("p u c n -> p (u c n)")[:, (c - 5) * NCOL:(c - 4) * NCOL] for c in range(DC)]
        hT_hi = [w_uq_r[:].rearrange("p m h q -> p (m h q)").rearrange("p (m t) -> p m t", m=4), qk_r[:]]
        CHUNKS = (2, 3, 4, 5, 6, 7, 0, 1)
        COLS = (slice(COL_CQ, NCOL), slice(0, COL_CQ))
        first_rows = [t[0:1].rearrange("p j n -> p (j n)") for t in (a_sb, v_sb)]

        d_small, d_mid, d_uq, d_out = sem("d_small"), sem("d_mid"), sem("d_uq"), sem("d_out")
        d_in = [sem("d_in_keys"), sem("d_in_rest")]
        s_in_hi, s_in_lo, s_hT_hi = sem("s_in_hi"), [sem("s_in_lo_keys"), sem("s_in_lo_rest")], sem("s_hT_hi")
        d_ada = [sem(f"d_ada{n}") for n in range(AHEAD)]
        d_row = [sem("d_row0"), sem("d_row1")]
        s_cond, s_link, s_alink = sem("s_cond"), sem("s_link"), sem("s_alink")
        s_unit, s_modps, s_mod = sem("s_unit"), sem("s_modps"), sem("s_mod")
        s_h, s_hTps, s_hT = sem("s_h"), sem("s_hTps"), sem("s_hT")
        s_rot, s_av, s_ave, s_vg = sem("s_rot"), sem("s_av"), sem("s_ave"), sem("s_vg")
        s_proj, s_u = sem("s_proj"), sem("s_u")
        s_sq, s_ssq, s_root, s_norm = sem("s_sq"), sem("s_ssq"), sem("s_root"), sem("s_norm")
        s_vn, s_wsT, s_wsTe, s_mixed, s_sg = sem("s_vn"), sem("s_wsT"), sem("s_wsTe"), sem("s_mixed"), sem("s_sg")
        s_dT, s_dTe, s_yT, s_yTe = sem("s_dT"), sem("s_dTe"), sem("s_yT"), sem("s_yTe")
        s_vatt, s_vatte = sem("s_vatt"), sem("s_vatte")
        s_qk, s_k, s_qn, s_q, s_kpe = sem("s_qk"), sem("s_k"), sem("s_qn"), sem("s_q"), sem("s_kpe")
        s_oe, s_S, s_max, s_exp, s_PT, s_PTe, s_O = sem("s_oe"), sem("s_S"), sem("s_max"), sem("s_exp"), sem("s_PT"), sem("s_PTe"), sem("s_O")
        s_w_hi, s_w_lo, s_mix_hi, s_mix_lo = sem("s_w_hi"), sem("s_w_lo"), sem("s_mix_hi"), sem("s_mix_lo")
        s_o, s_oT, s_y, s_x, s_wp0 = sem("s_o"), sem("s_oT"), sem("s_y"), sem("s_x"), sem("s_wp0")

        ada_src = dram("w_ada", l).rearrange("o (p c) n -> p (o c) n", c=DC)
        N_SOFT = HEADS * TJ

        with nc.Block() as block:
            @block.sync
            def _(sp):
                def ada(u):
                    q, half = u // 2, u % 2
                    at, n, _ = ada_unit(u)
                    if u >= AHEAD:
                        sp.wait_ge(s_unit, u - 1 if u >= AHEAD + 2 else u - AHEAD + 1)
                    sp.dma_start(at, ada_src[:, half * 4:half * 4 + 4, q * 512:q * 512 + 512]).then_inc(d_ada[n], 16)

                def ada_row(q):
                    wait(sp, s_modps, q - 1 if q >= 6 else 0)
                    sp.dma_start(b_row[:, q % 2, :], dram("b_ada", l)[:, q * 512:q * 512 + 512]).then_inc(d_row[q % 2], 16)

                sp.dma_start(cond[:, 0, :], ins["c"].rearrange("o (p c) -> p (o c)", c=DC)).then_inc(d_small, 16)
                sp.dma_start(first_rows[0], dram("b_ada", l)[:, 0:1024]).then_inc(d_small, 16)
                sp.dma_start(first_rows[1], dram("b_ada", l)[:, 1024:2048]).then_inc(d_small, 16)
                for u in range(8):
                    ada(u)
                for g, cols in enumerate((slice(COL_CQ, NIN), slice(0, COL_CQ))):
                    sp.dma_start(w_in[:, :, cols], dram("w_in", l).rearrange("o (p c) n -> p (o c) n", c=DC)[:, :, cols]).then_inc(d_in[g], 16)
                sp.dma_start(w_ukv[:].rearrange("p h q -> p (h q)"), dram("w_ukv", l).rearrange("o p n -> p (o n)")).then_inc(d_mid, 16)
                sp.dma_start(w_sp[:], dram("w_spatial", l).rearrange("o h t k -> t (o h) k")).then_inc(d_mid, 16)
                sp.dma_start(b_sp[:], dram("b_spatial", l)).then_inc(d_mid, 16)
                with nc.allow_non_contiguous_dma(reason="short vectors, a feature to a partition"):
                    sp.dma_start(pool_scale[:], dram("pool_scale", l).rearrange("o (m p) -> p (o m)", p=P)).then_inc(d_mid, 16)
                    sp.dma_start(g_q[:], dram("g_q", l).rearrange("o (m p) -> p (o m)", p=P)).then_inc(d_mid, 16)
                    sp.dma_start(g_kv[:], dram("g_kv", l).rearrange("o p -> p o")).then_inc(d_mid, 16)
                sp.wait_ge(s_wp0, 1)
                for g in range(2):
                    sp.dma_start(w_pool[64 * g:64 * g + 64, :, 64 * g:64 * g + 64],
                                 dram("w_pool", l).rearrange("o (m g) c d -> g c (o m) d", g=2)[g]).then_inc(d_mid, 16)
                sp.wait_ge(s_proj, 6)
                sp.wait_ge(s_av, TJ)
                for m in range(2):
                    sp.dma_start(w_uq[:, m, :, 0:QK], dram("w_uq", l).rearrange("o (m p) (h q) -> m p (o h) q", p=P, q=QK)[m]).then_inc(d_uq, 16)
                for q in range(4, 12):
                    ada(2 * q)
                    ada_row(q)
                    ada(2 * q + 1)
                    for m in range(2 * (q - 4), min(2 * (q - 4) + 2, DC)):
                        sp.dma_start(w_out[:, m, :], dram("w_out", l).rearrange("o (m p) n -> m p (o n)", p=P)[m]).then_inc(d_out, 16)

            @block.gpsimd
            def _(pool):
                pool.memset(w_pool[:], 0.0).then_inc(s_wp0, 1)
                half = ROPE // 2
                pool.wait_ge(d_in[0], 16)
                pool.tensor_scalar(w_in[:, :, NIN:NIN + half], w_in[:, :, COL_PE + half:COL_PE + ROPE], -1.0, 0.0, ALU.mult, ALU.add)
                pool.tensor_copy(w_in[:, :, NIN + half:NIN + ROPE], w_in[:, :, COL_PE:COL_PE + half]).then_inc(s_rot, 1)
                for n, c in enumerate(CHUNKS):
                    pool.wait_ge(s_in_hi, n + 1)
                    pool.tensor_tensor(w_in_r[:, c, COLS[0]], w_in[:, c, COLS[0]], w_in_hi[c][:, COLS[0]].bitcast(F32), ALU.subtract).then_inc(s_in_lo[0], 1)
                pool.wait_ge(d_uq, 32)
                for m in range(2):
                    pool.tensor_scalar(w_uq[:, m, :, QK:QK + half], w_uq[:, m, :, NOPE + half:QK], -1.0, 0.0, ALU.mult, ALU.add)
                    i = pool.tensor_copy(w_uq[:, m, :, QK + half:QK + ROPE], w_uq[:, m, :, NOPE:NOPE + half])
                i.then_inc(s_rot, 1)
                for n in range(2 * DC):
                    b, m = n // DC, n % DC
                    pool.wait_ge(s_w_hi, n + 1)
                    part = w_out[:, m, 512 * b:512 * b + 512]
                    pool.tensor_tensor(w_out_lo[:, m, 512 * b:512 * b + 512], part, w_out_hi[b][m].bitcast(F32), ALU.subtract).then_inc(s_w_lo, 1)

            @block.scalar
            def _(act):
                act.wait_ge(d_small, 48)
                act.activation(cond[:, 1, :], cond[:, 0, :], ACT.Silu).then_inc(s_cond, 1)

                def mod_out(q):
                    act.wait_ge(s_modps, q + 1)
                    bias = 1.0 if q // 2 in (SCALE1, 4) else 0.0
                    act.activation(mod[:, q // 2, (q % 2) * 512:(q % 2) * 512 + 512], bank[7][:], ACT.Copy, bias=bias).then_inc(s_mod, 1)

                def in_hi(g, c):
                    act.activation(w_in_hi[c][:, COLS[g]], w_in[:, c, COLS[g]], ACT.Copy).then_inc(s_in_hi, 1)

                for q in range(4):
                    mod_out(q)
                act.wait_ge(s_rot, 1)
                act.wait_ge(s_unit, 8)
                for c in CHUNKS[0:6]:
                    in_hi(0, c)
                for j in range(TJ):
                    act.wait_ge(s_hTps, j + 1)
                    for b in range(2):
                        i = act.activation(hT_hi[b][:, :, j * P:j * P + P],
                                           bank[2 * j + b][:].rearrange("p (c t) -> p c t", c=4), ACT.Copy)
                    i.then_inc(s_hT_hi, 1)
                    if j == 2:
                        act.wait_ge(s_h, TJ)
                        for c in CHUNKS[6:8]:
                            in_hi(0, c)
                act.wait_ge(d_in[1], 16)
                for c in CHUNKS:
                    in_hi(1, c)
                def gate_value(j):
                    act.wait_ge(s_ave, j + 1)
                    act.activation(v_sb[:, j, :], bank[4 + j % 2][:, 256:512], ACT.Gelu_apprx_tanh).then_inc(s_vg, 1)

                for n in range(2):
                    act.wait_ge(s_ssq, n + 1)
                    act.activation(tmp[:, n, :], bank[(7, 3)[n]][:], ACT.Sqrt, bias=cst("eps"), scale=1.0 / (QL if n == 0 else P)).then_inc(s_root, 1)
                for j in range(TJ):
                    gate_value(j)
                for m in range(2):
                    act.wait_ge(s_proj, m + 4)
                    act.activation(mixT[:, 2 + m, :], bank[m][:], ACT.Gelu_apprx_tanh).then_inc(s_u, 1)
                for j in range(TJ):
                    act.wait_ge(s_vn, j + 1)
                    act.activation(bn[:, j, 3:4], bn[:, j, 1:2], ACT.Sqrt, bias=cst("eps")).then_inc(s_root, 1)
                for j in range(TJ):
                    act.wait_ge(s_vatt, j + 1)
                    act.activation(hT[:, j, :], bank[4 + j % 2][:], ACT.Copy).then_inc(s_vatte, 1)
                for m in range(2):
                    act.wait_ge(s_yT, m + 1)
                    act.mul(mixT[:, m, :], bank[2 + m][:], pool_scale[:, m:m + 1]).then_inc(s_yTe, 1)

                def head_out(hd):
                    act.wait_ge(s_qk, hd + 1)
                    if hd >= 2:
                        act.wait_ge(s_S, (hd - 1) * TJ)
                    act.activation(q_sb[0:NOPE, hd % 2, :], bank[hd % 2][0:NOPE, :], ACT.Copy).then_inc(s_qn, 1)
                    act.activation(k_sb[0:NOPE, hd % 2, :], bank[2][0:NOPE, :], ACT.Copy).then_inc(s_k, 1)

                def pt(n):
                    hd, i = n // TJ, n % TJ
                    act.wait_ge(s_PT, n + 1)
                    if n >= 2:
                        act.wait_ge(s_O, n - 1)
                    act.activation(probsT[:, n % 2, 0:(i + 1) * P], bank[5][:, 0:(i + 1) * P], ACT.Copy).then_inc(s_PTe, 1)
                    if i == 0 and hd >= 1:
                        o_out(hd - 1)

                def o_out(hd):
                    act.wait_ge(s_O, (hd + 1) * TJ)
                    act.activation(o_att.rearrange("p i (h d) -> p i h d", d=VDIM)[:, :, hd, :],
                                    bank[6][:, 0:256].rearrange("p (i d) -> p i d", i=TJ), ACT.Copy).then_inc(s_oe, 1)

                def weight_hi(b, m):
                    act.wait_ge(d_out, 16 * DC)
                    act.activation(w_out_hi[b][m], w_out[:, m, 512 * b:512 * b + 512], ACT.Copy).then_inc(s_w_hi, 1)

                head_out(0)
                n = 0
                for hd in range(HEADS):
                    for i in range(TJ):
                        act.wait_ge(s_max, n + 1)
                        if n >= 2:
                            act.wait_ge(s_PT, n - 1)
                        act.activation(probs[:, n % 2, 0:(i + 1) * P], bank[3 + n % 2][:, 0:(i + 1) * P], ACT.Exp,
                                       scale=SCALE, bias=rs[:, N_SOFT + n:N_SOFT + n + 1],
                                       accum_out=rs[:, 2 * N_SOFT + n:2 * N_SOFT + n + 1]).then_inc(s_exp, 1)
                        if n >= 1:
                            pt(n - 1)
                        n += 1
                        if i == 2 and hd + 1 < HEADS:
                            head_out(hd + 1)
                        if i == 3 and hd >= 1:
                            mod_out(3 + hd)
                        if hd == HEADS - 2:
                            weight_hi(0, 2 * i)
                            weight_hi(0, 2 * i + 1)
                        if hd == HEADS - 1:
                            act.activation(mix_hi[0][:, i, :], mixT[:, i, :], ACT.Copy).then_inc(s_mix_hi, 1)
                pt(n - 1)
                o_out(HEADS - 1)
                mod_out(11)
                for m in range(DC):
                    weight_hi(1, m)
                for i in range(TJ):
                    act.wait_ge(s_oT, i + 1)
                    act.activation(mix_hi[1][:, :, i * P:i * P + P], bank[(5, 7)[i % 2]][:].rearrange("p (m t) -> p m t", m=4), ACT.Copy).then_inc(s_mix_hi, 1)
                for j in range(TJ):
                    act.wait_ge(s_x, TJ + j + 1)
                    act.activation(h[:, 0, :], x[:, j, :], ACT.Square, accum_out=stat[:, 16 + j:17 + j]).then_inc(s_alink, 1)
                    act.wait_ge(s_alink, j + 1)
                act.activation(stat[:, 20:24], stat[:, 16:20], ACT.Sqrt, bias=cst("eps"), scale=1.0 / D).then_inc(s_alink, 1)

            @block.vector
            def _(dve):
                links = [0]

                def link(i):
                    links[0] += 1
                    i.then_inc(s_link, 1)
                    dve.wait_ge(s_link, links[0])

                def ada(q, some=range(DC)):
                    for k in some:
                        u, c = 2 * q + k // 4, k % 4
                        if k == 0:
                            if q < 1:
                                dve.wait_ge(s_cond, 1)
                            wait(dve, s_modps, q - 1)
                        if c == 0:
                            _, n, count = ada_unit(u)
                            dve.wait_ge(d_ada[n], count)
                        w, by = ada_unit(u)[0][:, c, :], cond[:, 1, k:k + 1]
                        if k == 0:
                            i = dve.tensor_scalar(acc[:, q % 2, :], w, by, None, ALU.mult)
                        else:
                            i = dve.scalar_tensor_tensor(out=acc[:, q % 2, :], in0=w, scalar=by, in1=acc[:, q % 2, :], op0=ALU.mult, op1=ALU.add)
                        if c < 3:
                            link(i)
                        else:
                            i.then_inc(s_unit, 1)
                            dve.wait_ge(s_unit, u + 1)

                for q in range(4):
                    ada(q)
                link(dve.reciprocal(stat[:, 8:12], stat[:, 20:24]))
                dve.wait_ge(s_mod, 4)
                def normed(j):
                    wait(dve, s_hTps, j - 1)
                    link(dve.scalar_tensor_tensor(out=h[:, j % 2, :], in0=x[:, j, :], scalar=stat[:, 8 + j:9 + j], in1=mod[:, SCALE1, :], op0=ALU.mult, op1=ALU.mult))
                    dve.tensor_tensor(h[:, j % 2, :], h[:, j % 2, :], mod[:, SHIFT1, :], ALU.add).then_inc(s_h, 1)

                def turned_lo(j):
                    dve.wait_ge(s_hT_hi, j + 1)
                    for b in range(2):
                        i = dve.tensor_tensor(hT_r[:, 4 * b:4 * b + 4, j * P:j * P + P], bank[2 * j + b][:].rearrange("p (c t) -> p c t", c=4),
                                              hT_hi[b][:, :, j * P:j * P + P].bitcast(F32), ALU.subtract)
                    i.then_inc(s_hT, 1)

                for j in range(TJ):
                    normed(j)
                for j in range(TJ):
                    turned_lo(j)
                for n, c in enumerate(CHUNKS):
                    dve.wait_ge(s_in_hi, DC + n + 1)
                    dve.tensor_tensor(w_in_r[:, c, COLS[1]], w_in[:, c, COLS[1]], w_in_hi[c][:, COLS[1]].bitcast(F32), ALU.subtract).then_inc(s_in_lo[1], 1)
                for m in range(3):
                    dve.wait_ge(s_proj, m + 1)
                    link(dve.tensor_copy(latent[:, m, :], bank[m][:]))
                    dve.tensor_tensor(mixT[:, 4 + m, :], latent[:, m, :], latent[:, m, :], ALU.mult).then_inc(s_sq, 1)

                def pool_in(j):
                    dve.wait_ge(s_av, j + 1)
                    dve.tensor_copy(a_sb[:, j, :], bank[4 + j % 2][:, 0:256]).then_inc(s_ave, 1)

                pool_in(0)
                pool_in(1)
                for n in range(2):
                    dve.wait_ge(s_root, n + 1)
                    link(dve.reciprocal(tmp[:, n, :], tmp[:, n, :]))
                pool_in(2)
                pool_in(3)
                dve.wait_ge(d_mid, 16 * 8)
                for m in range(3):
                    g = g_q[:, m:m + 1] if m < 2 else g_kv[:, 0:1]
                    i = dve.scalar_tensor_tensor(out=latent[:, m, :], in0=latent[:, m, :], scalar=g, in1=tmp[:, m // 2, :], op0=ALU.mult, op1=ALU.mult)
                i.then_inc(s_norm, 1)
                for j in range(TJ):
                    dve.wait_ge(s_vg, j + 1)
                    link(dve.bn_stats(rs[:, 8 * j:8 * j + 6], v_sb[:, j, :]))
                    dve.bn_aggr(bn[:, j, 0:2], rs[:, 8 * j:8 * j + 6]).then_inc(s_vn, 1)
                dve.wait_ge(s_proj, 6)
                R, ROT = slice(NOPE, QK), slice(QK, QK + ROPE)
                link(dve.tensor_tensor(k_pe[R, 0, :], bank[3][R, :], cos[R, :], ALU.mult))
                link(dve.tensor_tensor(k_pe[R, 1, :], bank[3][ROT, :], sin[ROT, :], ALU.mult))
                for b in range(2):
                    i = dve.tensor_tensor(k_sb[R, b, :], k_pe[R, 0, :], k_pe[R, 1, :], ALU.add)
                i.then_inc(s_kpe, 1)
                for j in range(TJ):
                    dve.wait_ge(s_root, 3 + j)
                    link(dve.reciprocal(bn[:, j, 4:5], bn[:, j, 3:4]))
                    dve.tensor_scalar(v_sb[:, j, :], v_sb[:, j, :], bn[:, j, 0:1], bn[:, j, 4:5], ALU.subtract, ALU.mult).then_inc(s_vn, 1)
                dve.wait_ge(s_wsT, 1)
                dve.tensor_tensor(w_spT[:], bank[7][:].rearrange("p (h t) -> p h t", h=SGH),
                                  cst("upto").unsqueeze(1).to_broadcast([P, SGH, P]), ALU.mult).then_inc(s_wsTe, 1)
                for m in range(2):
                    dve.wait_ge(s_dT, m + 1)
                    dve.tensor_copy(dT[:, m, :], bank[2 + m][:]).then_inc(s_dTe, 1)
                for m in range(2):
                    dve.wait_ge(s_mixed, m + 1)
                    dve.wait_ge(s_u, 2)
                    dve.tensor_tensor(mixT[:, 2 + m, :], mixT[:, 2 + m, :], bank[m][:], ALU.mult).then_inc(s_sg, 1)
                dve.wait_ge(s_yT, 2)

                def rotate(hd):
                    dve.wait_ge(s_qk, hd + 1)
                    if hd >= 2:
                        dve.wait_ge(s_S, (hd - 1) * TJ)
                    dve.wait_ge(s_qn, hd + 1)
                    link(dve.tensor_tensor(tmp[R, 0, :], bank[hd % 2][R, :], cos[R, :], ALU.mult))
                    link(dve.tensor_tensor(tmp[R, 1, :], bank[hd % 2][ROT, :], sin[ROT, :], ALU.mult))
                    dve.tensor_tensor(q_sb[R, hd % 2, :], tmp[R, 0, :], tmp[R, 1, :], ALU.add).then_inc(s_q, 1)

                def mixed_lo(m):
                    dve.wait_ge(s_mix_hi, m + 1)
                    dve.tensor_tensor(mix_lo[:, m, :], mixT[:, m, :], mix_hi[0][:, m, :].bitcast(F32), ALU.subtract).then_inc(s_mix_lo, 1)

                rotate(0)
                n = 0
                for hd in range(HEADS):
                    for i in range(TJ):
                        dve.wait_ge(s_S, n + 1)
                        link(dve.reduce_max(rs[:, n:n + 1], bank[3 + n % 2][:, 0:(i + 1) * P], AX))
                        dve.tensor_scalar(rs[:, N_SOFT + n:N_SOFT + n + 1], rs[:, n:n + 1], -SCALE, None, ALU.mult).then_inc(s_max, 1)
                        if i == 3 and hd + 1 < HEADS:
                            rotate(hd + 1)
                        ada(4 + hd, (range(0, 3), range(3, 5), range(5, 8), ())[i])
                        if hd == HEADS - 1 and i >= 1:
                            mixed_lo(i - 1)
                        n += 1
                mixed_lo(TJ - 1)
                dve.wait_ge(s_exp, N_SOFT)
                link(dve.reciprocal(rs[:, 3 * N_SOFT:4 * N_SOFT], rs[:, 2 * N_SOFT:3 * N_SOFT]))
                dve.wait_ge(s_oe, HEADS)
                sums = rs[:, 3 * N_SOFT:4 * N_SOFT].rearrange("p (h i) -> p h i", i=TJ)
                for i in range(TJ):
                    dst = o_att[:, i, :].rearrange("p (h d) -> p h d", d=VDIM)
                    dve.tensor_tensor(dst, dst, sums[:, :, i].unsqueeze(2).to_broadcast([P, HEADS, VDIM]), ALU.mult).then_inc(s_o, 1)
                for i in range(TJ):
                    dve.wait_ge(s_mix_hi, 5 + i)
                    dve.tensor_tensor(mix_lo[:, 4:8, i * P:i * P + P], bank[(5, 7)[i % 2]][:].rearrange("p (m t) -> p m t", m=4),
                                      mix_hi[1][:, :, i * P:i * P + P].bitcast(F32), ALU.subtract).then_inc(s_mix_lo, 1)
                dve.wait_ge(s_mod, 6)
                for b in range(2):
                    for j in range(TJ):
                        n = TJ * b + j
                        dve.wait_ge(s_y, n + 1)
                        link(dve.tensor_tensor(tmp[:, n % 2, :], bank[n % 4][:], mod[:, GATE1, b * 512:b * 512 + 512], ALU.mult))
                        dve.tensor_tensor(x[:, j, b * 512:b * 512 + 512], x[:, j, b * 512:b * 512 + 512], tmp[:, n % 2, :], ALU.add).then_inc(s_x, 1)

            @block.tensor
            def _(pe):
                def ada(q):
                    pe.wait_ge(s_unit, 2 * q + 2)
                    if q >= 4:
                        pe.wait_ge(d_row[q % 2], 16 * (q // 2 - 1))
                        row = b_row[:, q % 2, :]
                    else:
                        pe.wait_ge(d_small, 48)
                        row = first_rows[q // 2][:, (q % 2) * 512:(q % 2) * 512 + 512]
                    wait(pe, s_mod, q)
                    pe.matmul(bank[7][:], ones, acc[:, q % 2, :], start=True, stop=False)
                    pe.matmul(bank[7][:], ones[0:1, :], row, start=False, stop=True).then_inc(s_modps, 1)

                for q in range(4):
                    ada(q)
                for j in range(TJ):
                    pe.wait_ge(s_h, j + 1)
                    if j == TJ - 1:
                        pe.wait_ge(s_mod, 4)
                    for c in range(DC):
                        i = pe.transpose(bank[2 * j + c // 4][:, (c % 4) * P:(c % 4) * P + P], h[:, j % 2, c:D:DC], ident)
                    i.then_inc(s_hTps, 1)
                def product(to, left, right, passes=((0, 0), (1, 0), (0, 1))):
                    for n, c in enumerate(CHUNKS):
                        a, b = left(c), right(c)
                        for p in passes:
                            i = pe.matmul(to, a[p[0]], b[p[1]], start=n == 0 and p == (0, 0), stop=n == DC - 1 and p == (0, 1))
                    return i

                def latent_rows(b, col, passes):
                    return product(bank[b][:], lambda c: (w_in_hi[c][:, col:col + P], w_in_r[:, c, col:col + P]),
                                   lambda c: h_part(c, slice(0, T)), passes)

                def h_part(c, tokens):
                    return hT_hi[c // 4][:, c % 4, tokens], hT_r[:, c, tokens]

                def feature_rows(b, col):
                    product(bank[b][:], lambda c: (w_in_hi[c][:, col:col + P], w_in_r[:, c, col:col + P]),
                            lambda c: h_part(c, slice(0, T))).then_inc(s_proj, 1)

                def token_rows(j):
                    if j >= 2:
                        pe.wait_ge(s_ave, j - 1)
                        pe.wait_ge(s_vg, j - 1)

                    def pool_and_values(w):
                        return w.rearrange("p (a b) -> p a b", b=512)[:, :, 0:256]

                    product(bank[4 + j % 2][:], lambda c: h_part(c, slice(j * P, j * P + P)),
                            lambda c: (pool_and_values(w_in_hi[c][:, 0:1024]), pool_and_values(w_in_r[:, c, 0:1024]))).then_inc(s_av, 1)

                pe.wait_ge(s_in_lo[0], DC)
                pe.wait_ge(s_hT_hi, TJ)
                for b, col in enumerate((COL_CQ, COL_CQ + P, COL_CKV)):
                    pe.wait_ge(s_hT, 1 if b < 2 else 2)
                    latent_rows(b, col, ((0, 0), (1, 0)))
                pe.wait_ge(s_hT, TJ)
                for b, col in enumerate((COL_CQ, COL_CQ + P, COL_CKV)):
                    latent_rows(b, col, ((0, 1),)).then_inc(s_proj, 1)
                pe.wait_ge(s_in_lo[1], DC)
                token_rows(0)
                pe.wait_ge(s_sq, 3)
                pe.wait_ge(s_mod, 4)
                pe.matmul(bank[7][:], ones, mixT[:, 4, :], start=True, stop=False)
                pe.matmul(bank[7][:], ones, mixT[:, 5, :], start=False, stop=True).then_inc(s_ssq, 1)
                pe.matmul(bank[3][:], ones, mixT[:, 6, :], start=True, stop=True).then_inc(s_ssq, 1)
                token_rows(1)
                for b in range(2):
                    feature_rows(b, COL_U + b * P)
                token_rows(2)
                token_rows(3)
                pe.wait_ge(s_root, 2)
                feature_rows(3, COL_PE - NOPE)
                pe.wait_ge(d_mid, 16 * 8)
                pe.wait_ge(s_root, 2)
                for hd in range(SGH):
                    i = pe.transpose(bank[7][:, hd * P:hd * P + P], w_sp[:, hd, :], ident)
                i.then_inc(s_wsT, 1)
                pe.wait_ge(s_ave, TJ)
                at = CONST["band"][0]
                for m in range(2):
                    if m == 1:
                        pe.wait_ge(s_kpe, 1)
                    for gg in range(2):
                        g = 2 * m + gg
                        for j in range(TJ):
                            dst = bank[2 + m][64 * gg:64 * gg + 64, j * P:j * P + P]
                            kind = 0 if j == 0 else 1
                            i = pe.matmul(dst, a_sb[:, j, g * 64:g * 64 + 64], const[:, at + (g * 3 + kind) * P:at + (g * 3 + kind + 1) * P],
                                          start=True, stop=j == 0)
                            if j:
                                i = pe.matmul(dst, a_sb[:, j - 1, g * 64:g * 64 + 64], const[:, at + (g * 3 + 2) * P:at + (g * 3 + 3) * P],
                                              start=False, stop=True)
                    i.then_inc(s_dT, 1)
                pe.wait_ge(s_norm, 1)
                for j in range(TJ):
                    pe.wait_ge(s_vg, TJ)
                    wait(pe, s_vatte, j - 1)
                    pe.matmul(bank[4 + j % 2][:], latent[:, 2, j * P:j * P + P], w_ukv[:, :, NOPE:], start=True, stop=True).then_inc(s_vatt, 1)
                pe.wait_ge(s_vn, 2 * TJ)
                pe.wait_ge(s_wsTe, 1)
                pe.wait_ge(s_u, 2)
                for m in range(2):
                    for gg in range(2):
                        hd = 2 * m + gg
                        for j in range(TJ):
                            dst = bank[m][64 * gg:64 * gg + 64, j * P:j * P + P]
                            pe.matmul(dst, v_sb[:, j, hd * 64:hd * 64 + 64], w_spT[:, hd, :], start=True, stop=False)
                            i = pe.matmul(dst, ones[0:1, 0:64], b_sp[:, hd, :], start=False, stop=True)
                    i.then_inc(s_mixed, 1)
                for m in range(2):
                    pe.wait_ge(s_dTe, m + 1)
                    pe.matmul(bank[2 + m][:], w_pool[:, m, :], dT[:, m, :], start=True, stop=True).then_inc(s_yT, 1)

                def project(hd):
                    if hd == 0:
                        pe.wait_ge(s_rot, 2)
                        pe.wait_ge(s_sg, 2)
                        pe.wait_ge(s_yTe, 2)
                        pe.wait_ge(s_vatte, TJ)
                    else:
                        wait(pe, s_q, hd - 1)
                        pe.wait_ge(s_k, hd)
                    for m in range(2):
                        pe.matmul(bank[hd % 2][:], w_uq[:, m, hd, :], latent[:, m, :], start=m == 0, stop=m == 1)
                    pe.matmul(bank[2][0:NOPE, :], w_ukv[:, hd, 0:NOPE], latent[:, 2, :], start=True, stop=True).then_inc(s_qk, 1)

                def scores(n):
                    hd, i = n // TJ, n % TJ
                    pe.wait_ge(s_q, hd + 1)
                    pe.wait_ge(s_k, hd + 1)
                    if n >= 2:
                        pe.wait_ge(s_exp, n - 1)
                    dst = bank[3 + n % 2]
                    pe.matmul(dst[:, 0:(i + 1) * P], q_sb[:, hd % 2, i * P:i * P + P], k_sb[:, hd % 2, 0:(i + 1) * P], start=True, stop=False)
                    pe.matmul(dst[:, i * P:i * P + P], identb[:], causalb[:], start=False, stop=True).then_inc(s_S, 1)

                def turn(n):
                    i = n % TJ
                    pe.wait_ge(s_exp, n + 1)
                    wait(pe, s_PTe, n)
                    for k in range(i + 1):
                        ins_ = pe.transpose(bank[5][:, k * P:k * P + P], probs[:, n % 2, k * P:k * P + P], ident)
                    ins_.then_inc(s_PT, 1)

                def attend(n):
                    hd, i = n // TJ, n % TJ
                    pe.wait_ge(s_PTe, n + 1)
                    if i == 0 and hd >= 1:
                        pe.wait_ge(s_oe, hd)
                    at = i * VDIM
                    for k in range(i + 1):
                        ins_ = pe.matmul(bank[6][:, at:at + VDIM], probsT[:, n % 2, k * P:k * P + P], v_att[:, k, hd, :],
                                         start=k == 0, stop=k == i)
                    ins_.then_inc(s_O, 1)

                project(0)
                scores(0)
                for n in range(N_SOFT):
                    if n + 1 < N_SOFT:
                        scores(n + 1)
                    turn(n)
                    if n % TJ == 1 and n // TJ + 1 < HEADS:
                        project(n // TJ + 1)
                    if n % TJ == 2 and n >= TJ:
                        ada(3 + n // TJ)
                    if n >= 1:
                        attend(n - 1)
                attend(N_SOFT - 1)
                ada(3 + HEADS)

                def mixed_out(b, j, chunks):
                    for m in chunks:
                        hi, lo = mix_hi[m // 4][:, m % 4, j * P:j * P + P], mix_lo[:, m, j * P:j * P + P]
                        w_hi, w_lo = w_out_hi[b][m], w_out_lo[:, m, b * 512:b * 512 + 512]
                        to = bank[(TJ * b + j) % 4][:]
                        pe.matmul(to, hi, w_hi, start=m == 0, stop=False)
                        pe.matmul(to, hi, w_lo, start=False, stop=False)
                        i = pe.matmul(to, lo, w_hi, start=False, stop=m == DC - 1)
                    return i

                pe.wait_ge(s_mix_lo, 4)
                pe.wait_ge(s_w_lo, DC)
                for j in range(TJ):
                    mixed_out(0, j, range(0, 4))
                for i in range(TJ):
                    pe.wait_ge(s_o, i + 1)
                    if i >= 2:
                        pe.wait_ge(s_mix_lo, 4 + i - 1)
                    else:
                        pe.wait_ge(s_mod, 12)
                    for m in range(4):
                        ins_ = pe.transpose(bank[(5, 7)[i % 2]][:, m * P:m * P + P], o_att[:, i, m * P:m * P + P], ident)
                    ins_.then_inc(s_oT, 1)
                for j in range(TJ):
                    pe.wait_ge(s_mix_lo, 4 + j + 1)
                    mixed_out(0, j, range(4, 8)).then_inc(s_y, 1)
                pe.wait_ge(s_w_lo, 2 * DC)
                for j in range(TJ):
                    pe.wait_ge(s_x, j + 1)
                    mixed_out(1, j, range(DC)).then_inc(s_y, 1)
        clear(nc, sems)


def experts(nc, ins, l, v):
    cst, x, mod, h, hT, mixT, stat, bank, dram = (v[k] for k in "cst x mod h hT mixT stat bank dram".split())
    ident, ones, cum_pairs = v["ident"], v["ones"], v["cum_pairs"]
    h2_dram, y_dram, gathered_dma, scattered_dma = v["h2_dram"], v["y_dram"], v["gathered_dma"], v["scattered_dma"]
    SHIFT2, SCALE2, GATE2 = 3, 4, 5
    with ExitStack() as stack:
        def sb(name, shape, dt=F32):
            return stack.enter_context(nc.sbuf_tensor(name, shape, dt))

        sems = []

        def sem(name):
            sems.append(stack.enter_context(nc.semaphore(name)))
            return sems[-1]

        raw_gu = [sb(f"raw_gu{i}", [P, 2, DC, FF]) for i in range(2)]
        raw_d = [sb(f"raw_d{i}", [P, 2, D]) for i in range(2)]
        meta = sb("meta", [P, TJ, E, 3])
        rank = sb("rank", [P, E, TJ])
        listed = sb("listed", [P, NTAB, 3])
        rank_off = sb("rank_off", [P, NTAB])
        block_expert = sb("block_expert", [1, NTAB], I32)
        block_rows = sb("block_rows", [1, NTAB], I32)
        more_pairs = sb("more_pairs", [1, 1], I32)
        gidx = [sb(f"gidx{i}", [P, 1], I32) for i in range(2)]
        sidx = [sb(f"sidx{i}", [P, 1], I32) for i in range(2)]
        with ExitStack() as early:
            def sbe(name, shape):
                return early.enter_context(nc.sbuf_tensor(name, shape, F32))

            ws_g, ws_u, ws_d = sbe("ws_g", [P, DC, FF]), sbe("ws_u", [P, DC, FF]), sbe("ws_d", [P, 2, D])
            w_router, bias = sbe("w_router_sb", [P, DC, E]), sbe("router_bias_sb", [P, E])
            rt = sbe("rt", [P, 8, TJ, E])
            cnt = sbe("cnt", [P, 3, P])
            small = sbe("small", [P, 64])
            chosenT = sbe("chosenT", [P, TJ, P])
            top = sbe("top", [P, TJ * NG, 8])
            sbe("unused", [P, 256])
            act_sT, act_s, sil_s = sbe("act_sT", [P, 2, P]), sbe("act_s", [P, TJ, FF]), sbe("sil_s", [P, FF])
        w_hi = [sb(f"w_hi{n}", [P, 4, 2, FF], F32R) for n in "ab"] + [sb("w_hid", [P, 2, D], F32R)]
        w_lo = [sb(f"w_lo{n}", [P, 4, 2, FF], F32R) for n in "ab"] + [sb("w_lod", [P, 2, D], F32R)]
        hbT_hi, hbT_lo = sb("hbT_hi", [P, DC, P], F32R), sb("hbT_lo", [P, DC, P], F32R)
        actT_hi, actT_lo = sb("actT_hi", [P, 2, P], F32R), sb("actT_lo", [P, 2, P], F32R)
        h2 = [h[:, 0, :], h[:, 1, :]] + [mixT[:, 4 + 2 * i:6 + 2 * i, :].rearrange("p a n -> p (a n)") for i in range(2)]
        hb = [mixT[:, 2 * i:2 * i + 2, :].rearrange("p a n -> p (a n)") for i in range(2)]
        yb = [mixT[:, 4 + 2 * i:6 + 2 * i, :].rearrange("p a n -> p (a n)") for i in range(2)]
        sel = h[:, 0, 512:1024].rearrange("p (j s) -> p j s", j=TJ)
        shared_y = h[:, :, 0:512]
        act_b, sil_b = hT[:, 1, 0:FF], hT[:, 2, 0:FF]

        s_w = sem("s_w")
        d_ws = sem("d_ws")
        s_link, s_h, s_hTps, s_hT = (sem(n) for n in "s_link s_h s_hTps s_hT".split())
        s_h2 = sem("s_h2")
        s_logit, s_score, s_M, s_MT, s_MTe, s_ranks = (sem(n) for n in "s_logit s_score s_M s_MT s_MTe s_ranks".split())
        s_count, s_nb, s_cum, s_cume, s_tab, s_table = (sem(n) for n in "s_count s_nb s_cum s_cume s_tab s_table".split())
        s_sgu, s_ssil, s_sact, s_sT, s_sTe, s_sdown, s_sx = (sem(n) for n in "s_sgu s_ssil s_sact s_sT s_sTe s_sdown s_sx".split())
        y_part = [raw_gu[k // 2][:, k % 2].rearrange("p c f -> p (c f)").rearrange("p (k n) -> p k n", k=2) for k in range(4)]
        s_zero, s_started = sem("s_zero"), sem("s_started")
        raw_gu_in, raw_d_in = [sem("raw_gu_in0"), sem("raw_gu_in1")], [sem("raw_d_in0"), sem("raw_d_in1")]
        hi = [sem("hi_a"), sem("hi_b"), sem("hi_d")]
        lo = [sem("lo_a"), sem("lo_b"), sem("lo_d")]
        s_gu_half, s_gu, s_down, s_turn, s_list, s_actT = (sem(n) for n in "s_gu_half s_gu s_down s_turn s_list s_actT".split())
        s_hb_hi, s_hb_lo, s_sil, s_act, s_aT_hi, s_aT_lo = (sem(n) for n in "s_hb_hi s_hb_lo s_sil s_act s_aT_hi s_aT_lo".split())
        s_yout, s_sel, s_gidx, s_sidx, s_gathered, s_scattered = (sem(n) for n in "s_yout s_sel s_gidx s_sidx s_gathered s_scattered".split())
        y_in = [sem(f"y_in{k}") for k in range(4)]
        s_xout = sem("s_xout")
        s_ysum, s_square = sem("s_ysum"), sem("s_square")

        h2_rows = h2_dram.rearrange("(j p) n -> p j n", p=P)
        y_rows = y_dram.rearrange("(k j p) n -> p k j n", p=P, j=TJ)
        wg, wu, wd = ins["w_gate"], ins["w_up"], ins["w_down"]
        bank_s = [bank[4], bank[6]]
        bank_g, bank_t, bank_y, bank_a, bank_l = bank[0:2], bank[2:4], bank[4:6], bank[6], bank[7]

        def expert_of(eng, s):
            return eng.value_load(block_expert[0:1, bass.ds(s.n, 1)], min_val=0, max_val=E - 1)

        def steps(eng, step):
            for n in range(3):
                step(Step(n // 2, n % 2))
            more = eng.value_load(more_pairs[0:1, 0:1], min_val=MIN_PAIRS - LEAST, max_val=MAX_PAIRS - LEAST) + (LEAST - 1)
            with eng.Fori(0, RUNS) as run:
                with eng.If(run * RUN + 1 < more):
                    with eng.Fori(0, RUN) as k:
                        with eng.If(run * RUN + k + 1 < more):
                            i = run * RUN + k + 1
                            step(Step(i, 1))
                            step(Step(i + 1, 0))
            step(Step(more, 1), last=True)
            return Step(more + 1, 0)

        with nc.Block() as block:
            @block.sync
            def _(sp):
                sp.dma_start(w_router[:], dram("w_router", l).rearrange("o (p c) e -> p (o c) e", c=DC)).then_inc(s_w, 16)
                sp.dma_start(bias[:], dram("router_bias", l).to_broadcast([P, E])).then_inc(s_w, 16)
                sp.dma_start(ws_g[:], dram("ws_gate", l).rearrange("o (p c) f -> p (o c) f", c=DC)).then_inc(d_ws, 16)
                sp.dma_start(ws_u[:], dram("ws_up", l).rearrange("o (p c) f -> p (o c) f", c=DC)).then_inc(d_ws, 16)
                sp.dma_start(ws_d[:], dram("ws_down", l).rearrange("o (p c) n -> p (o c) n", c=2)).then_inc(d_ws, 16)
                for j in range(TJ):
                    sp.wait_ge(s_h, j + 1)
                    sp.dma_start(h2_rows[:, j, :], h2[j]).then_inc(s_h2, 16)
                sp.wait_ge(s_table, 1)

                def load_gate_up(s):
                    at = (bass.ds(l, 1), bass.ds(expert_of(sp, s), 1))
                    wait(sp, lo[1], s.n - 1)
                    for k, w in enumerate((wg, wu)):
                        sp.dma_start(raw_gu[s.par][:, k], w[at].rearrange("a b (p c) f -> p (a b c) f", c=DC)).then_inc(raw_gu_in[s.par], 16)

                def load_down(s):
                    at = (bass.ds(l, 1), bass.ds(expert_of(sp, s), 1))
                    wait(sp, lo[2], s.n - 1)
                    sp.dma_start(raw_d[s.par][:], wd[at].rearrange("a b (p c) n -> p (a b c) n", c=2)).then_inc(raw_d_in[s.par], 16)

                def step(s, last=False):
                    if not last:
                        load_gate_up(s + 1)
                    load_down(s)

                load_gate_up(Step(0, 0))
                sp.wait_ge(s_started, 1)
                end = steps(sp, step)
                sp.wait_ge(s_scattered, end.n)
                for u in range(4 * TJ):
                    wait(sp, s_ysum, u - 3)
                    sp.dma_start(y_part[u % 4], y_rows[:, 2 * (u % 4):2 * (u % 4) + 2, u // 4, :]).then_inc(y_in[u % 4], 16)

            @block.gpsimd
            def _(pool):
                bound_h, bound_y = pool.to_reg(T - 1), pool.to_reg(TOPK * T - 1)
                for i in range(2):
                    pool.memset(hb[i], 0.0).then_inc(s_zero, 1)
                pool.wait_ge(s_zero, 2)
                pool.wait_ge(s_h2, 16 * TJ)
                before = pool.snap(cum_pairs, min_val=0, max_val=DEPTH * (MAX_PAIRS + 1))

                def by_rows(s, move):
                    rows = pool.value_load(block_rows[0:1, bass.ds(s.n, 1)], min_val=0, max_val=T)

                    def halve(sizes):
                        if len(sizes) == 1:
                            move(sizes[0])
                            return
                        mid = len(sizes) // 2
                        with pool.If(rows < sizes[mid - 1] + 1):
                            halve(sizes[:mid])
                        with pool.Else():
                            halve(sizes[mid:])

                    halve(MOVED)

                def gather(s):
                    wait(pool, s_turn, s.n - 1)
                    pool.wait_ge(s_gidx, s.n + 1)
                    pool.nop().then_inc(s_started, 1)
                    by_rows(s, lambda rows: pool.indirect_dma_start(
                        out=hb[s.par][0:rows], out_offset=None, in_=h2_dram,
                        in_offset=bass.IndirectOffsetOnAxis(ap=gidx[s.par][0:rows, 0:1].bitcast(U32), axis=0),
                        bounds_check=bound_h, oob_is_err=False).then_inc(gathered_dma[s.par], 16))

                def gathered(s):
                    pool.wait_ge(gathered_dma[s.par], (before + s.half + 1 + (l if s.par == 0 else 0)) * 16)
                    pool.nop().then_inc(s_gathered, 1)

                def scatter(s):
                    pool.wait_ge(s_sidx, s.n + 1)
                    pool.wait_ge(s_yout, s.n + 1)
                    pool.nop().then_inc(s_started, 1)
                    by_rows(s, lambda rows: pool.indirect_dma_start(
                        out=y_dram, in_=yb[s.par][0:rows], in_offset=None,
                        out_offset=bass.IndirectOffsetOnAxis(ap=sidx[s.par][0:rows, 0:1].bitcast(U32), axis=0),
                        bounds_check=bound_y, oob_is_err=False).then_inc(scattered_dma[s.par], 16))

                def scattered(s):
                    pool.wait_ge(scattered_dma[s.par], (before + s.half + 1) * 16)
                    pool.nop().then_inc(s_scattered, 1)

                gather(Step(0, 0))
                gather(Step(0, 1))

                def step(s, last=False):
                    gathered(s + 1)
                    if not last:
                        gather(s + 2)
                    if later(s, 2):
                        scattered(s + -2)
                    if later(s, 1):
                        scatter(s + -1)

                gathered(Step(0, 0))
                end = steps(pool, step)
                scattered(end + -2)
                scatter(end + -1)
                scattered(end + -1)
                pool.reg_add(cum_pairs, cum_pairs, pool.to_reg(end.half))

            @block.scalar
            def _(act):
                for j in range(TJ):
                    act.wait_ge(s_hTps, j + 1)
                    for b in range(2):
                        i = act.activation(hT[:, 4 * b:4 * b + 4, j * P:j * P + P],
                                           bank[2 * (j % 2) + b][:].rearrange("p (c t) -> p c t", c=4), ACT.Copy)
                    i.then_inc(s_hT, 1)
                act.wait_ge(s_logit, 1)
                act.activation(rt[:, 0], bank[4][:, 0:TJ * E].rearrange("p (j e) -> p j e", j=TJ), ACT.Sigmoid).then_inc(s_score, 1)
                for j in range(TJ):
                    act.wait_ge(s_sgu, j + 1)
                    wait(act, s_sact, j)
                    act.activation(sil_s[:], bank[j % 2][:, 0:FF], ACT.Silu).then_inc(s_ssil, 1)

                def shared_turned(j):
                    act.wait_ge(s_sT, j + 1)
                    wait(act, s_sdown, 2 * j)
                    act.activation(act_sT[:], bank[5][:, 0:2 * P].rearrange("p (c t) -> p c t", c=2), ACT.Copy).then_inc(s_sTe, 1)

                def part_hi(k, s):
                    act.wait_ge((raw_gu_in, raw_gu_in, raw_d_in)[k][s.par], (s.half + 1) * (32 if k < 2 else 16))
                    if k < 2:
                        act.activation(w_hi[k][:].rearrange("p c g f -> p g c f"), raw_gu[s.par][:, :, 4 * k:4 * k + 4, :], ACT.Copy).then_inc(hi[k], 1)
                    else:
                        act.activation(w_hi[2][:], raw_d[s.par][:], ACT.Copy).then_inc(hi[2], 1)

                def turned_hi(s):
                    act.wait_ge(s_turn, s.n + 1)
                    wait(act, s_gu, s.n)
                    for b in range(2):
                        i = act.activation(hbT_hi[:, 4 * b:4 * b + 4, :], bank_t[b][:].rearrange("p (c t) -> p c t", c=4), ACT.Copy)
                    i.then_inc(s_hb_hi, 1)

                def y_out(s):
                    act.wait_ge(s_down, s.n + 1)
                    wait(act, s_scattered, s.n - 1)
                    for b in range(2):
                        i = act.activation(yb[s.par][:, 512 * b:512 * b + 512], bank_y[b][:], ACT.Copy)
                    i.then_inc(s_yout, 1)

                shared_turned(0)
                shared_turned(1)
                part_hi(0, Step(0, 0))
                part_hi(1, Step(0, 0))
                turned_hi(Step(0, 0))
                shared_turned(2)
                shared_turned(3)

                def step(s, last=False):
                    if last:
                        y_out(s + -1)
                        part_hi(2, s)
                    act.wait_ge(s_gu_half, s.n + 1)
                    if not last:
                        part_hi(0, s + 1)
                    act.wait_ge(s_gu, s.n + 1)
                    wait(act, s_act, s.n)
                    act.activation(sil_b, bank_g[s.par][:, 0:FF], ACT.Silu).then_inc(s_sil, 1)
                    if not last:
                        part_hi(1, s + 1)
                        turned_hi(s + 1)
                        if later(s, 1):
                            y_out(s + -1)
                        part_hi(2, s)
                    act.wait_ge(s_actT, s.n + 1)
                    act.activation(actT_hi[:], bank_a[:, 0:2 * P].rearrange("p (c t) -> p c t", c=2), ACT.Copy).then_inc(s_aT_hi, 1)

                end = steps(act, step)
                y_out(end + -1)
                for j in range(TJ):
                    act.wait_ge(s_xout, j + 1)
                    act.activation(h[:, 1, :], x[:, j, :], ACT.Square, accum_out=stat[:, 16 + j:17 + j]).then_inc(s_square, 1)
                    act.wait_ge(s_square, j + 1)
                act.activation(stat[:, 20:24], stat[:, 16:20], ACT.Sqrt, bias=cst("eps"), scale=1.0 / D).then_inc(s_square, 1)

            @block.vector
            def _(dve):
                links = [0]

                def link(i):
                    links[0] += 1
                    i.then_inc(s_link, 1)
                    dve.wait_ge(s_link, links[0])

                link(dve.reciprocal(stat[:, 8:12], stat[:, 20:24]))
                for j in range(TJ):
                    link(dve.scalar_tensor_tensor(out=h2[j], in0=x[:, j, :], scalar=stat[:, 8 + j:9 + j], in1=mod[:, SCALE2, :], op0=ALU.mult, op1=ALU.mult))
                    dve.tensor_tensor(h2[j], h2[j], mod[:, SHIFT2, :], ALU.add).then_inc(s_h, 1)

                def shared_act(j):
                    dve.wait_ge(s_ssil, j + 1)
                    dve.tensor_tensor(act_s[:, j, :], bank[j % 2][:, FF:2 * FF], sil_s[:], ALU.mult).then_inc(s_sact, 1)

                def shared_sum(j):
                    for b in range(2):
                        dve.wait_ge(s_sdown, 2 * j + b + 1)
                        link(dve.tensor_tensor(shared_y[:, b, :], bank_s[b][:], mod[:, GATE2, 512 * b:512 * b + 512], ALU.mult))
                        dve.tensor_tensor(x[:, j, 512 * b:512 * b + 512], x[:, j, 512 * b:512 * b + 512], shared_y[:, b, :], ALU.add).then_inc(s_sx, 1)

                score, sel_score, junk, chosen, weight, left = (rt[:, k] for k in range(6))
                grouped = [P, TJ, NG, PER_G]

                def by_group(a):
                    return a.rearrange("p j (g e) -> p j g e", g=NG)

                dve.wait_ge(s_score, 1)
                dve.wait_ge(s_w, 32)
                link(dve.tensor_tensor(sel_score, score, bias[:].unsqueeze(1).to_broadcast([P, TJ, E]), ALU.add))
                for j in range(TJ):
                    for g in range(NG):
                        i = dve.max(top[:, j * NG + g, :], sel_score[:, j, g * PER_G:g * PER_G + PER_G])
                link(i)
                group = small[:, 0:TJ * NG].rearrange("p (j g) -> p j g", j=TJ)
                link(dve.tensor_tensor(small[:, 0:TJ * NG], top[:, :, 0], top[:, :, 1], ALU.add))
                better, ties = junk, left
                this = group.unsqueeze(3).to_broadcast(grouped)
                for j in range(TJ):
                    this, other = group[:, j, :].unsqueeze(2).to_broadcast([P, NG, NG]), group[:, j, :].unsqueeze(1).to_broadcast([P, NG, NG])
                    dve.tensor_tensor(by_group(better)[:, j], other, this, ALU.is_gt)
                    i = dve.tensor_tensor(by_group(ties)[:, j], other, this, ALU.is_equal)
                link(i)
                link(dve.tensor_tensor(ties, ties, cst("lower_group").unsqueeze(1).to_broadcast([P, TJ, E]), ALU.mult))
                link(dve.tensor_tensor(better, better, ties, ALU.add))
                keep = small[:, 32:64].rearrange("p (j g) -> p j g", j=TJ)
                link(dve.tensor_reduce(small[:, 32:64], better.rearrange("p j (g e) -> p (j g) e", g=NG), AX, ALU.add))
                link(dve.tensor_scalar(small[:, 32:64], small[:, 32:64], float(TOPG), None, ALU.is_lt))
                link(dve.tensor_scalar(small[:, 0:32], small[:, 32:64], -MASKED, MASKED, ALU.mult, ALU.add))

                def spread(a):
                    return a.rearrange("p (q o) -> p q o", o=1).to_broadcast([P, TJ * NG, PER_G])

                flat = [a.rearrange("p j (g e) -> p (j g) e", g=NG) for a in (sel_score, left)]
                link(dve.tensor_tensor(flat[0], flat[0], spread(small[:, 32:64]), ALU.mult))
                link(dve.tensor_tensor(flat[0], flat[0], spread(small[:, 0:32]), ALU.add))
                for j in range(TJ):
                    link(dve.max(top[:, j, :], sel_score[:, j, :]))
                    i = dve.match_replace(out=left[:, j, :], in_to_replace=top[:, j, :], in_values=sel_score[:, j, :], imm_value=TAKEN)
                link(i)
                dve.tensor_scalar(chosen, left, (TAKEN + MASKED) / 2, None, ALU.is_lt).then_inc(s_M, 1)
                dve.wait_ge(s_M, 1)
                link(dve.tensor_tensor(weight, score, chosen, ALU.mult))
                link(dve.tensor_reduce(small[:, 0:TJ], weight, AX, ALU.add))
                link(dve.reciprocal(small[:, 4:8], small[:, 0:TJ]))
                link(dve.tensor_scalar(small[:, 4:8], small[:, 4:8], 2.5, None, ALU.mult))
                dve.tensor_tensor(meta[:, :, :, 2], weight, small[:, 4:8].unsqueeze(2).to_broadcast([P, TJ, E]), ALU.mult)
                shared_act(0)
                shared_act(1)
                dve.wait_ge(s_count, 1)
                link(dve.tensor_scalar(small[0:E, 8:12], cst("steps", E), bank[5][0:E, 256:257], None, ALU.is_lt))
                link(dve.tensor_copy(small[0:E, 14:15], bank[5][0:E, 256:257]))
                link(dve.tensor_reduce(small[0:E, 12:13], small[0:E, 8:12], AX, ALU.add))
                dve.tensor_scalar(cnt[0:E, 0, :], ones[0:E, :], small[0:E, 12:13], None, ALU.mult).then_inc(s_nb, 1)
                dve.wait_ge(s_MT, 1)
                dve.tensor_copy(chosenT[0:E], bank[7][0:E, :].rearrange("p (j t) -> p j t", j=TJ)).then_inc(s_MTe, 1)
                dve.wait_ge(s_cum, 1)
                link(dve.tensor_copy(small[0:E, 13:14], bank[5][0:E, 257:258]))
                link(dve.tensor_tensor(small[0:E, 15:16], small[0:E, 13:14], small[0:E, 12:13], ALU.subtract))
                link(dve.tensor_scalar(cnt[0:E, 2, 0:NTAB], cst("block", E), small[0:E, 15:16], None, ALU.is_ge))
                link(dve.tensor_scalar(cnt[0:E, 1, 0:NTAB], cst("block", E), small[0:E, 13:14], None, ALU.is_ge))
                dve.tensor_tensor(cnt[0:E, 2, 0:NTAB], cnt[0:E, 2, 0:NTAB], cnt[0:E, 1, 0:NTAB], ALU.subtract).then_inc(s_cume, 1)
                dve.wait_ge(s_ranks, 1)
                for j in range(TJ):
                    link(dve.tensor_tensor(junk[:, j, :], bank[6][:, j * E:j * E + E], chosen[:, j, :], ALU.mult))
                link(dve.tensor_scalar(left, chosen, -NO_SLOT, NO_SLOT, ALU.mult, ALU.add))
                link(dve.tensor_tensor(rank[:].rearrange("p e j -> p j e"), junk, left, ALU.add))
                dve.wait_ge(s_tab, 1)
                link(dve.tensor_scalar(cnt[:, 2, 0:NTAB], bank[7][:, 0:NTAB], float(E), None, ALU.is_equal))
                link(dve.tensor_scalar(small[:, 16:17], bank[7][:, 2 * P:2 * P + 1], 0.0, None, ALU.add))
                link(dve.tensor_scalar(rt[:, 7].rearrange("p j e -> p (j e)")[:, 0:NTAB], bank[7][:, 0:NTAB], float(E - 1), None, ALU.min))
                link(dve.tensor_copy(block_expert[:], rt[0:1, 7].rearrange("p j e -> p (j e)")[:, 0:NTAB]))
                link(dve.tensor_tensor(rank_off[:], cst("block"), bank[7][:, P:P + NTAB], ALU.subtract))
                link(dve.scalar_tensor_tensor(out=rank_off[:], in0=cnt[:, 2, 0:NTAB], scalar=64.0, in1=rank_off[:], op0=ALU.mult, op1=ALU.add))
                link(dve.tensor_scalar(rank_off[:], rank_off[:], float(P), None, ALU.mult))
                link(dve.tensor_tensor(cnt[0:1, 2, 0:NTAB], bank[7][0:1, 3 * P:3 * P + NTAB], rank_off[0:1, :], ALU.subtract))
                link(dve.tensor_scalar(block_rows[:], cnt[0:1, 2, 0:NTAB], 0.0, None, ALU.max))
                link(dve.tensor_scalar(cnt[:, 2, 0:MAX_PAIRS + 1], cst("even"), small[:, 16:17], None, ALU.is_lt))
                link(dve.tensor_reduce(small[:, 17:18], cnt[:, 2, 0:MAX_PAIRS + 1], AX, ALU.add))
                link(dve.tensor_scalar(more_pairs[:], small[0:1, 17:18], -float(LEAST), None, ALU.add))
                dve.wait_ge(s_ranks, 2)
                for j in range(TJ):
                    dve.tensor_scalar(meta[:, j, :, 1], bank[4][:, j * E:j * E + E], float(T), cst("token")[:, j:j + 1], ALU.mult, ALU.add)
                    i = dve.tensor_scalar(meta[:, j, :, 0], chosen[:, j, :], 0.0, cst("token")[:, j:j + 1], ALU.mult, ALU.add)
                i.then_inc(s_table, 1)
                def select(s):
                    e = expert_of(dve, s)
                    wait(dve, s_list, s.n)
                    dve.scalar_tensor_tensor(out=sel, in0=cst("slots").unsqueeze(1).to_broadcast([P, TJ, P]),
                                             scalar=rank_off[:, bass.ds(s.n, 1)],
                                             in1=rank[:, bass.ds(e, 1), :].rearrange("p e j -> p (e j)").unsqueeze(2).to_broadcast([P, TJ, P]),
                                             op0=ALU.add, op1=ALU.is_equal).then_inc(s_sel, 1)

                def listing(s):
                    dve.wait_ge(s_list, s.n + 1)
                    wait(dve, s_gathered, s.n - 1)
                    dve.tensor_copy(listed[:, bass.ds(s.n, 1), :].rearrange("p b k -> p (b k)"), bank_l[:, 0:3])
                    dve.tensor_scalar(gidx[s.par][:], bank_l[:, 0:1], NO_SLOT, None, ALU.add).then_inc(s_gidx, 1)

                def part_lo(k, s):
                    dve.wait_ge(hi[k], s.n + 1)
                    if k < 2:
                        dve.tensor_tensor(w_lo[k][:].rearrange("p c g f -> p g c f"), raw_gu[s.par][:, :, 4 * k:4 * k + 4, :],
                                          w_hi[k][:].bitcast(F32).rearrange("p c g f -> p g c f"), ALU.subtract).then_inc(lo[k], 1)
                    else:
                        dve.tensor_tensor(w_lo[2][:], raw_d[s.par][:], w_hi[2][:].bitcast(F32), ALU.subtract).then_inc(lo[2], 1)

                def turned_lo(s):
                    dve.wait_ge(s_hb_hi, s.n + 1)
                    for b in range(2):
                        i = dve.tensor_tensor(hbT_lo[:, 4 * b:4 * b + 4, :], bank_t[b][:].rearrange("p (c t) -> p c t", c=4),
                                              hbT_hi[:, 4 * b:4 * b + 4, :].bitcast(F32), ALU.subtract)
                    i.then_inc(s_hb_lo, 1)

                dve.wait_ge(s_h2, 16 * TJ)
                for n in range(2):
                    select(Step(0, n))
                    shared_act(2 + n)
                    listing(Step(0, n))
                select(Step(1, 0))
                shared_sum(0)
                part_lo(0, Step(0, 0))
                shared_sum(1)
                part_lo(1, Step(0, 0))
                turned_lo(Step(0, 0))
                shared_sum(2)
                shared_sum(3)

                def step(s, last=False):
                    if not last:
                        part_lo(0, s + 1)
                        listing(s + 2)
                    else:
                        part_lo(2, s)
                    dve.wait_ge(s_sil, s.n + 1)
                    wait(dve, s_actT, s.n)
                    dve.wait_ge(s_gidx, s.n + 1)
                    dve.scalar_tensor_tensor(out=act_b, in0=bank_g[s.par][:, FF:2 * FF], scalar=listed[:, bass.ds(s.n, 1), 2],
                                             in1=sil_b, op0=ALU.mult, op1=ALU.mult).then_inc(s_act, 1)
                    if not last:
                        turned_lo(s + 1)
                        part_lo(1, s + 1)
                        select(s + 3)
                        part_lo(2, s)
                    dve.wait_ge(s_aT_hi, s.n + 1)
                    dve.tensor_tensor(actT_lo[:], bank_a[:, 0:2 * P].rearrange("p (c t) -> p c t", c=2), actT_hi[:].bitcast(F32), ALU.subtract).then_inc(s_aT_lo, 1)
                    wait(dve, s_scattered, s.n - 1)
                    dve.tensor_scalar(sidx[s.par][:], listed[:, bass.ds(s.n, 1), 1], NO_SLOT, None, ALU.add).then_inc(s_sidx, 1)

                steps(dve, step)
                for j in range(TJ):
                    for k in range(4):
                        part = y_part[k]
                        dve.wait_ge(y_in[k], 16 * (j + 1))
                        if k == 0:
                            dve.tensor_tensor(yb[0], part[:, 0], part[:, 1], ALU.add).then_inc(s_ysum, 1)
                        else:
                            link(dve.tensor_tensor(yb[0], yb[0], part[:, 0], ALU.add))
                            dve.tensor_tensor(yb[0], yb[0], part[:, 1], ALU.add).then_inc(s_ysum, 1)
                        dve.wait_ge(s_ysum, 4 * j + k + 1)
                    link(dve.tensor_tensor(yb[0], yb[0], mod[:, GATE2, :], ALU.mult))
                    dve.tensor_tensor(x[:, j, :], x[:, j, :], yb[0], ALU.add).then_inc(s_xout, 1)
                    dve.wait_ge(s_xout, j + 1)

            @block.tensor
            def _(pe):
                def turn_tokens(j):
                    pe.wait_ge(s_h, j + 1)
                    wait(pe, s_hT, j - 1)
                    for c in range(DC):
                        i = pe.transpose(bank[2 * (j % 2) + c // 4][:, (c % 4) * P:(c % 4) * P + P], h2[j][:, c:D:DC], ident)
                    i.then_inc(s_hTps, 1)

                def logits(j):
                    pe.wait_ge(s_hT, j + 1)
                    for c in range(DC):
                        i = pe.matmul(bank[4][:, j * E:j * E + E], hT[:, c, j * P:j * P + P], w_router[:, c, :], start=c == 0, stop=c == DC - 1)
                    return i

                turn_tokens(0)
                pe.wait_ge(s_w, 32)
                for j in range(1, TJ):
                    turn_tokens(j)
                    logits(j - 1)
                logits(TJ - 1).then_inc(s_logit, 1)

                def shared(j):
                    wait(pe, s_sact, j - 1)
                    for k, w in enumerate((ws_g, ws_u)):
                        for c in range(DC):
                            i = pe.matmul(bank[j % 2][:, k * FF:k * FF + FF], hT[:, c, j * P:j * P + P], w[:, c, :], start=c == 0, stop=c == DC - 1)
                    i.then_inc(s_sgu, 1)

                def shared_down(j):
                    pe.wait_ge(s_sact, j + 1)
                    wait(pe, s_sTe, j)
                    for c in range(2):
                        i = pe.transpose(bank[5][:, c * P:c * P + P], act_s[:, j, c:FF:2], ident)
                    i.then_inc(s_sT, 1)
                    pe.wait_ge(s_sTe, j + 1)
                    for b in range(2):
                        wait(pe, s_sx, 2 * (j - 1) + b + 1)
                        for c in range(2):
                            i = pe.matmul(bank_s[b][:], act_sT[:, c, :], ws_d[:, c, 512 * b:512 * b + 512], start=c == 0, stop=c == 1)
                        i.then_inc(s_sdown, 1)

                pe.wait_ge(d_ws, 48)
                shared(0)
                shared(1)
                chosen = rt[:, 3]
                pe.wait_ge(s_M, 1)
                for j in range(TJ):
                    i = pe.matmul(bank[5][0:E, 256:257], chosen[:, j, :], ones[:, 0:1], start=j == 0, stop=j == TJ - 1)
                i.then_inc(s_count, 1)
                for j in range(TJ):
                    for k in range(j + 1):
                        i = pe.matmul(bank[6][:, j * E:j * E + E], cst("before") if k == j else ones, chosen[:, k, :], start=k == 0, stop=k == j)
                i.then_inc(s_ranks, 1)
                for j in range(TJ):
                    i = pe.transpose(bank[7][0:E, j * P:j * P + P], chosen[:, j, :], ident)
                i.then_inc(s_MT, 1)
                pe.wait_ge(s_nb, 1)
                pe.matmul(bank[5][0:E, 257:258], cst("upto", E)[:, 0:E], cnt[0:E, 0, 0:1], start=True, stop=True).then_inc(s_cum, 1)
                shared(2)
                pe.wait_ge(s_MTe, 1)
                pe.wait_ge(s_score, 1)
                for j in range(TJ):
                    i = pe.matmul(bank[4][:, j * E:j * E + E], chosenT[0:E, j, :], cst("before", E)[:, 0:E], start=True, stop=True)
                i.then_inc(s_ranks, 1)
                pe.wait_ge(s_cume, 1)
                pe.matmul(bank[7][:, 0:NTAB], ones[0:E, :], cnt[0:E, 1, 0:NTAB], start=True, stop=True)
                pe.matmul(bank[7][:, P:P + NTAB], cnt[0:E, 0, :], cnt[0:E, 1, 0:NTAB], start=True, stop=True)
                pe.matmul(bank[7][0:1, 3 * P:3 * P + NTAB], small[0:E, 14:15], cnt[0:E, 2, 0:NTAB], start=True, stop=True)
                pe.matmul(bank[7][:, 2 * P:2 * P + 1], cnt[0:E, 0, :], ones[0:E, 0:1], start=True, stop=True).then_inc(s_tab, 1)
                shared(3)

                def list_block(s):
                    e = expert_of(pe, s)
                    pe.wait_ge(s_sel, s.n + 1)
                    wait(pe, s_gidx, s.n)
                    for j in range(TJ):
                        i = pe.matmul(bank_l[:, 0:3], sel[:, j, :], meta[:, j, bass.ds(e, 1), :].rearrange("p e k -> p (e k)"), start=j == 0, stop=j == TJ - 1)
                    i.then_inc(s_list, 1)

                def turn(s):
                    pe.wait_ge(s_gathered, s.n + 1)
                    wait(pe, s_hb_lo, s.n)
                    for c in range(DC):
                        i = pe.transpose(bank_t[c // 4][:, (c % 4) * P:(c % 4) * P + P], hb[s.par][:, c:D:DC], ident)
                    i.then_inc(s_turn, 1)

                def product(dst, a_hi, a_lo, b_hi, b_lo, first, last):
                    pe.matmul(dst, a_hi, b_hi, start=first, stop=False)
                    pe.matmul(dst, a_hi, b_lo, start=False, stop=False)
                    return pe.matmul(dst, a_lo, b_hi, start=False, stop=last)

                def gate_up(s):
                    pe.wait_ge(s_hb_lo, s.n + 1)
                    wait(pe, s_act, s.n - 1)
                    for k in range(2):
                        pe.wait_ge(lo[k], s.n + 1)
                        for c in range(4):
                            cc = 4 * k + c
                            i = product(bank_g[s.par][:], hbT_hi[:, cc, :], hbT_lo[:, cc, :],
                                        w_hi[k][:, c].rearrange("p g f -> p (g f)"), w_lo[k][:, c].rearrange("p g f -> p (g f)"), cc == 0, cc == DC - 1)
                        i.then_inc((s_gu_half, s_gu)[k], 1)

                def down(s):
                    pe.wait_ge(s_aT_lo, s.n + 1)
                    pe.wait_ge(lo[2], s.n + 1)
                    wait(pe, s_yout, s.n)
                    for c in range(2):
                        for b in range(2):
                            w = slice(512 * b, 512 * b + 512)
                            i = product(bank_y[b][:], actT_hi[:, c, :], actT_lo[:, c, :], w_hi[2][:, c, w], w_lo[2][:, c, w], c == 0, c == 1)
                    i.then_inc(s_down, 1)

                def turn_act(s):
                    pe.wait_ge(s_act, s.n + 1)
                    wait(pe, s_aT_lo, s.n)
                    if not later(s, 1):
                        pe.wait_ge(s_sx, 2 * TJ)
                    for c in range(2):
                        i = pe.transpose(bank_a[:, c * P:c * P + P], act_b[:, c:FF:2], ident)
                    i.then_inc(s_actT, 1)

                pe.wait_ge(s_table, 1)
                list_block(Step(0, 0))
                shared_down(0)
                list_block(Step(0, 1))
                shared_down(1)
                turn(Step(0, 0))
                shared_down(2)
                shared_down(3)

                def step(s, last=False):
                    if last:
                        down(s + -1)
                    gate_up(s)
                    if not last:
                        list_block(s + 2)
                        turn(s + 1)
                        if later(s, 1):
                            down(s + -1)
                    turn_act(s)

                end = steps(pe, step)
                down(end + -1)
        clear(nc, sems)


_NAMES = ["x", "c", "positions", "w_ada", "b_ada", "w_in", "w_pool", "pool_scale", "w_spatial", "b_spatial", "g_q", "w_uq",
          "g_kv", "w_ukv", "w_out", "w_router", "router_bias", "w_gate", "w_up", "w_down", "ws_gate", "ws_up", "ws_down",
          "final_gain"]


def kernel(**inputs):
    import concourse.bacc as bacc
    from concourse.bass_utils import run_bass_kernel_spmd

    arrays = {n: np.ascontiguousarray(inputs[n]) for n in _NAMES}
    arrays["const"] = lay_constants()
    nc = bacc.Bacc("TRN2", target_bir_lowering=False, num_devices=1)
    ins = {n: nc.dram_tensor(f"in_{n}", a.shape, mybir.dt.from_np(a.dtype), kind="ExternalInput").ap() for n, a in arrays.items()}
    out = nc.dram_tensor("out_0", (1, T, D), F32, kind="ExternalOutput").ap()
    h2_rows = nc.dram_tensor("h2_rows", (T, D), F32, kind="Internal").ap()
    y_rows = nc.dram_tensor("y_rows", (TOPK * T, D), F32, kind="Internal").ap()
    trunk(nc, ins, out, (h2_rows, y_rows))
    r = run_bass_kernel_spmd(nc, [{f"in_{n}": a for n, a in arrays.items()}], core_ids=[0])
    return r.results[0]["out_0"]
```
